# Optimizing a Trainium2 kernel written in Bass

```python
import math
import jax, jax.numpy as jnp
from jax import lax
import numpy as np

D_MODEL = 2048
BATCH = 1
SEQ = 128
DEPTH = 1
DEC_BATCH = 1
DEC_SEQ = 512
PAST_LEN = 128

GRID_W = 64
D_RNN = 1024
RNN_BLOCKS = 8
RNN_BS = D_RNN // RNN_BLOCKS
CONV_W = 4
CONV_LEFT = 2
LRU_C = 8.0
N_HEADS = 8
HD = 64
VD = 2 * HD
QK_W = N_HEADS * 2 * HD
ATT_W = N_HEADS * VD
Q_BLOCK = 128
ROPE_BASE = 10000.0
ROPE_AXIS_DIM = HD // 2
N_EXPERTS = 16
D_EXPERT = 1024
EC_FACTOR = 2
EPS = 1e-6
IN_COLS = 2 * D_RNN + 2 * QK_W + ATT_W + 2 * D_MODEL
SPLITS = (D_RNN, 2 * D_RNN, 2 * D_RNN + QK_W, 2 * D_RNN + 2 * QK_W, 2 * D_RNN + 2 * QK_W + ATT_W)

kernel_name = 'hybrid_diffusion_rglru_diffattn_ec'

def rmsnorm(x, g):
    xf = x.astype(jnp.float32)
    r = xf * lax.rsqrt(jnp.mean(xf * xf, axis=-1, keepdims=True) + EPS)
    return (r * g.astype(jnp.float32)).astype(x.dtype)

def modulation(cvec, w_mod, b_mod):
    m = jax.nn.silu(cvec) @ w_mod + b_mod
    return m[..., None, :]

def centred_conv(x, w, b):
    n = x.shape[1]
    xp = jnp.pad(x, ((0, 0), (CONV_LEFT, CONV_W - 1 - CONV_LEFT), (0, 0)))
    out = xp[:, 0:n] * w[0]
    for tap in range(1, CONV_W):
        out = out + xp[:, tap:tap + n] * w[tap]
    return out + b

def block_diag(x, w, b):
    B, n, C = x.shape
    xb = x.reshape(B, n, RNN_BLOCKS, RNN_BS)
    y = jnp.einsum('bnki,kij->bnkj', xb, w.astype(x.dtype))
    return y.reshape(B, n, C) + b.astype(x.dtype)

def _lin_comb(left, right):
    a1, b1 = left
    a2, b2 = right
    return a1 * a2, a2 * b1 + b2

def rglru_bidir(xc, wr, br, wi, bi, lam, h0):
    xf = xc.astype(jnp.float32)
    ys = []
    finals = []
    for d, rev in ((0, False), (1, True)):
        r = jax.nn.sigmoid(block_diag(xf, wr[d], br[d]))
        i = jax.nn.sigmoid(block_diag(xf, wi[d], bi[d]))
        log_a = -LRU_C * r * jax.nn.softplus(-lam[d].astype(jnp.float32))
        a = jnp.exp(log_a)
        bterm = jnp.sqrt(-jnp.expm1(2.0 * log_a)) * (i * xf)
        ca, cb = lax.associative_scan(_lin_comb, (a, bterm), reverse=rev, axis=1)
        h = ca * h0[:, d, None, :].astype(jnp.float32) + cb
        ys.append(h)
        finals.append(h[:, 0] if rev else h[:, -1])
    y = ys[0] + ys[1]
    return y.astype(xc.dtype), jnp.stack(finals, axis=1)

def axial_rope(n):
    rows = n // GRID_W
    row = jnp.repeat(jnp.arange(rows), GRID_W).astype(jnp.float32)
    col = jnp.tile(jnp.arange(GRID_W), rows).astype(jnp.float32)
    inv = ROPE_BASE ** (-jnp.arange(0, ROPE_AXIS_DIM, 2, dtype=jnp.float32) / ROPE_AXIS_DIM)
    ang = jnp.concatenate([row[:, None] * inv, col[:, None] * inv], axis=-1)
    return jnp.cos(ang), jnp.sin(ang)

def apply_rope(x, cos, sin):
    cos = cos[None, :, None, None, :].astype(x.dtype)
    sin = sin[None, :, None, None, :].astype(x.dtype)
    x1 = x[..., :HD // 2]
    x2 = x[..., HD // 2:]
    return jnp.concatenate([x1 * cos - x2 * sin, x2 * cos + x1 * sin], axis=-1)

def diff_attn(q, k, v, lam):
    s = jnp.einsum('bqhcd,bkhcd->bhcqk', q, k).astype(jnp.float32) * (HD ** -0.5)
    p = jax.nn.softmax(s, axis=-1)
    pd = p[:, :, 0] - lam * p[:, :, 1]
    return jnp.einsum('bhqk,bkhd->bqhd', pd.astype(v.dtype), v)

def blocked_diff_attn(q, k, v, lam):
    B, n = q.shape[0], q.shape[1]
    nb = n // Q_BLOCK
    qb = q.reshape(B, nb, Q_BLOCK, N_HEADS, 2, HD).swapaxes(0, 1)
    ob = lax.map(lambda qi: diff_attn(qi, k, v, lam), qb)
    return ob.swapaxes(0, 1).reshape(B, n, N_HEADS, VD)

def token_mixer(h, lp, layer_idx, h0, ctx_k, ctx_v, rope):
    B, n, _ = h.shape
    proj = h @ lp['w_in']
    xr, gr, q, k, v, gates = jnp.split(proj, SPLITS, axis=-1)
    xc = centred_conv(xr, lp['conv_w'], lp['conv_b'])
    y, h_fin = rglru_bidir(xc, lp['lru_wr'], lp['lru_br'], lp['lru_wi'], lp['lru_bi'], lp['lru_lam'], h0)
    out_a = (y * jax.nn.gelu(gr)) @ lp['w_a_out']
    q = q.reshape(B, n, N_HEADS, 2, HD)
    k = k.reshape(B, n, N_HEADS, 2, HD)
    v = v.reshape(B, n, N_HEADS, VD)
    lam_init = 0.8 - 0.6 * math.exp(-0.3 * layer_idx)
    lam = (jnp.exp(jnp.sum(lp['lam_q1'].astype(jnp.float32) * lp['lam_k1'].astype(jnp.float32)))
           - jnp.exp(jnp.sum(lp['lam_q2'].astype(jnp.float32) * lp['lam_k2'].astype(jnp.float32)))
           + lam_init)
    if ctx_k is None:
        o = diff_attn(q, k, v, lam)
    else:
        q = apply_rope(q, *rope)
        k = apply_rope(k, *rope)
        k_all = jnp.concatenate([ctx_k.astype(k.dtype), k], axis=1)
        v_all = jnp.concatenate([ctx_v.astype(v.dtype), v], axis=1)
        o = blocked_diff_attn(q, k_all, v_all, lam)
    o = rmsnorm(o, lp['g_sub']) * (1.0 - lam_init)
    out_b = o.reshape(B, n, ATT_W) @ lp['w_b_out']
    ga, gb = jnp.split(jax.nn.sigmoid(gates), 2, axis=-1)
    out = (ga * out_a + gb * out_b) @ lp['w_o']
    return out, k.reshape(B, n, N_HEADS, 2 * HD), v, h_fin

def expert_choice_ffn(h, w_router, w_gate, w_up, w_down):
    B, n, D = h.shape
    cap = EC_FACTOR * n // N_EXPERTS
    aff = jax.nn.softmax((h @ w_router).astype(jnp.float32), axis=-1)
    vals, idx = lax.top_k(aff.swapaxes(1, 2), cap)
    xs = jax.vmap(lambda hb, ib: hb[ib])(h, idx)
    hid = jax.nn.silu(jnp.einsum('becd,edf->becf', xs, w_gate)) * jnp.einsum('becd,edf->becf', xs, w_up)
    ye = jnp.einsum('becf,efd->becd', hid, w_down) * vals[..., None].astype(h.dtype)
    return jax.vmap(lambda ib, yb: jnp.zeros((n, D), yb.dtype).at[ib.reshape(-1)].add(yb.reshape(-1, D)))(idx, ye)

def trunk_layer(x, mod, lp, layer_idx, h0, ctx_k, ctx_v, rope):
    sh1, sc1, g1, sh2, sc2, g2 = jnp.split(mod, 6, axis=-1)
    h = rmsnorm(x, lp['g_pre1']) * (1 + sc1) + sh1
    t, k, v, h_fin = token_mixer(h, lp, layer_idx, h0, ctx_k, ctx_v, rope)
    x = x + g1 * rmsnorm(t, lp['g_post1'])
    h = rmsnorm(x, lp['g_pre2']) * (1 + sc2) + sh2
    f = expert_choice_ffn(h, lp['w_router'], lp['w_e_gate'], lp['w_e_up'], lp['w_e_down'])
    x = x + g2 * rmsnorm(f, lp['g_post2'])
    return x, k, v, h_fin

def setup_inputs(seed: int = 0) -> dict:
    key = jax.random.key(seed)
    ks = jax.random.split(key, 40)
    f32 = jnp.float32

    def nrm(i, shape, scale):
        return jax.random.normal(ks[i], shape, f32) * scale

    u = jax.random.uniform(ks[39], (DEPTH, 2, D_RNN), f32, 0.9, 0.999)
    return {
        'x_prompt': nrm(0, (BATCH, SEQ, D_MODEL), 1.0),
        'x_sample': nrm(1, (DEC_BATCH, DEC_SEQ, D_MODEL), 1.0),
        'cache_k': nrm(2, (DEC_BATCH, DEPTH, PAST_LEN, N_HEADS, 2 * HD), 1.0),
        'cache_v': nrm(3, (DEC_BATCH, DEPTH, PAST_LEN, N_HEADS, VD), 1.0),
        'state_rnn': nrm(4, (DEC_BATCH, DEPTH, 2, D_RNN), 0.5),
        'c': nrm(5, (DEC_BATCH, D_MODEL), 1.0),
        'c_ctx': nrm(6, (D_MODEL,), 1.0),
        'w_mod': nrm(7, (DEPTH, D_MODEL, 6 * D_MODEL), 0.5 * D_MODEL ** -0.5),
        'b_mod': nrm(8, (DEPTH, 6 * D_MODEL), 0.01),
        'g_pre1': 1.0 + nrm(9, (DEPTH, D_MODEL), 0.05),
        'g_post1': 1.0 + nrm(10, (DEPTH, D_MODEL), 0.05),
        'g_pre2': 1.0 + nrm(11, (DEPTH, D_MODEL), 0.05),
        'g_post2': 1.0 + nrm(12, (DEPTH, D_MODEL), 0.05),
        'w_in': nrm(13, (DEPTH, D_MODEL, IN_COLS), D_MODEL ** -0.5),
        'conv_w': nrm(14, (DEPTH, CONV_W, D_RNN), 0.5),
        'conv_b': nrm(15, (DEPTH, D_RNN), 0.01),
        'lru_wr': nrm(16, (DEPTH, 2, RNN_BLOCKS, RNN_BS, RNN_BS), RNN_BS ** -0.5),
        'lru_br': nrm(17, (DEPTH, 2, D_RNN), 0.01),
        'lru_wi': nrm(18, (DEPTH, 2, RNN_BLOCKS, RNN_BS, RNN_BS), RNN_BS ** -0.5),
        'lru_bi': nrm(19, (DEPTH, 2, D_RNN), 0.01),
        'lru_lam': jnp.log(u) - jnp.log1p(-u),
        'lam_q1': nrm(20, (DEPTH, HD), 0.1),
        'lam_k1': nrm(21, (DEPTH, HD), 0.1),
        'lam_q2': nrm(22, (DEPTH, HD), 0.1),
        'lam_k2': nrm(23, (DEPTH, HD), 0.1),
        'g_sub': 1.0 + nrm(24, (DEPTH, VD), 0.05),
        'w_a_out': nrm(25, (DEPTH, D_RNN, D_MODEL), D_RNN ** -0.5),
        'w_b_out': nrm(26, (DEPTH, ATT_W, D_MODEL), ATT_W ** -0.5),
        'w_o': nrm(27, (DEPTH, D_MODEL, D_MODEL), D_MODEL ** -0.5),
        'w_router': nrm(28, (DEPTH, D_MODEL, N_EXPERTS), D_MODEL ** -0.5),
        'w_e_gate': nrm(29, (DEPTH, N_EXPERTS, D_MODEL, D_EXPERT), D_MODEL ** -0.5),
        'w_e_up': nrm(30, (DEPTH, N_EXPERTS, D_MODEL, D_EXPERT), D_MODEL ** -0.5),
        'w_e_down': nrm(31, (DEPTH, N_EXPERTS, D_EXPERT, D_MODEL), D_EXPERT ** -0.5),
    }

def reference(x_prompt, x_sample, cache_k, cache_v, state_rnn, c, c_ctx, w_mod, b_mod,
              g_pre1, g_post1, g_pre2, g_post2, w_in, conv_w, conv_b, lru_wr, lru_br,
              lru_wi, lru_bi, lru_lam, lam_q1, lam_k1, lam_q2, lam_k2, g_sub, w_a_out,
              w_b_out, w_o, w_router, w_e_gate, w_e_up, w_e_down):
    n_lat = x_sample.shape[1]
    rope = axial_rope(n_lat)
    B_ctx = x_prompt.shape[0]
    B_dec = x_sample.shape[0]
    L_past = cache_k.shape[2]

    xp = x_prompt
    xs = x_sample
    ks_out, vs_out, st_out = [], [], []
    for l in range(DEPTH):
        lp = {
            'g_pre1': g_pre1[l], 'g_post1': g_post1[l], 'g_pre2': g_pre2[l], 'g_post2': g_post2[l],
            'w_in': w_in[l], 'conv_w': conv_w[l], 'conv_b': conv_b[l],
            'lru_wr': lru_wr[l], 'lru_br': lru_br[l], 'lru_wi': lru_wi[l], 'lru_bi': lru_bi[l],
            'lru_lam': lru_lam[l], 'lam_q1': lam_q1[l], 'lam_k1': lam_k1[l],
            'lam_q2': lam_q2[l], 'lam_k2': lam_k2[l], 'g_sub': g_sub[l],
            'w_a_out': w_a_out[l], 'w_b_out': w_b_out[l], 'w_o': w_o[l],
            'w_router': w_router[l], 'w_e_gate': w_e_gate[l], 'w_e_up': w_e_up[l], 'w_e_down': w_e_down[l],
        }
        mod_ctx = modulation(c_ctx[None, :], w_mod[l], b_mod[l])
        h0_ctx = jnp.zeros((B_ctx, 2, D_RNN), jnp.float32)
        xp, k_c, v_c, h_c = trunk_layer(xp, mod_ctx, lp, l, h0_ctx, None, None, None)
        ks_out.append(k_c)
        vs_out.append(v_c)
        st_out.append(h_c.astype(state_rnn.dtype))
        mod_lat = modulation(c, w_mod[l], b_mod[l])
        ctx_k = cache_k[:, l].reshape(B_dec, L_past, N_HEADS, 2, HD)
        ctx_v = cache_v[:, l]
        xs, _, _, _ = trunk_layer(xs, mod_lat, lp, l, state_rnn[:, l], ctx_k, ctx_v, rope)

    new_cache_k = jnp.stack(ks_out, axis=1)
    new_cache_v = jnp.stack(vs_out, axis=1)
    new_state_rnn = jnp.stack(st_out, axis=1)
    return (xp, xs, new_cache_k, new_cache_v, new_state_rnn)


_drawn_inputs = setup_inputs


def setup_inputs(seed=0):
    import zlib

    import numpy as np

    out = dict(_drawn_inputs(seed))
    spreads = {}
    factors = {'g_post2': 4.088,
     'lru_br': 27.709,
     'lru_bi': 6.016,
     'lam_q1': 57.784,
     'lam_k1': 25.704,
     'lam_q2': 5.114,
     'lam_k2': 64.0,
     'g_sub': 3.523}
    for name, (base, spread) in spreads.items():
        noise = np.random.default_rng([zlib.crc32(name.encode()), seed]).standard_normal(out[name].shape)
        drawn = base * np.exp(spread * noise) if base else spread * noise
        out[name] = __import__('jax').numpy.asarray(drawn.astype(out[name].dtype))
    for name, factor in factors.items():
        out[name] = (out[name] * factor).astype(out[name].dtype)
    return out
```

```python
from contextlib import ExitStack

import numpy as np

import concourse.bass as bass
from concourse import mybir

F32 = mybir.dt.float32
F32R = mybir.dt.float32r
U32 = mybir.dt.uint32
ALU = mybir.AluOpType
ACT = mybir.ActivationFunctionType
AX = mybir.AxisListType

P = 128
D = 2048
N_LAT, N_CTX = 512, 128
N_TOK = N_LAT + N_CTX
TT = N_TOK // P
HALF = N_TOK // 2
KT = D // P
D_RNN = 1024
NB = D_RNN // P
NH, HD = 8, 64
PAST = 128
NKEY = PAST + N_LAT
NE = 16
D_EXP = 1024
CAP_LAT, CAP_CTX = 2 * N_LAT // NE, 2 * N_CTX // NE
CAP = CAP_LAT + CAP_CTX
EPS = 1e-6
ATT_SCALE = HD ** -0.5
LAM_INIT = 0.2
GRID_W = 64
V_COL, GATE_COL = 4096, 5120

NRAW = 4
NHL = 2
INC = 32
QUADS = [24, 2, 8, 8, 4, 4, NE * 6]
Q_MOD, Q_V, Q_IN, Q_GATE, Q_AB, Q_O, Q_EXP = (sum(QUADS[:i]) for i in range(7))

CW, CB, BR, BI, LAM_, H0, NEG = 0, 4, 5, 7, 9, 11, 13
NPRM = 15
N_PAR = 15
PER_HEAD = 51


def rope_tables():
    pos = np.arange(N_LAT)
    row, col = (pos // GRID_W).astype(np.float32), (pos % GRID_W).astype(np.float32)
    axis = HD // 2
    inv = (np.float32(10000.0) ** (-np.arange(0, axis, 2, dtype=np.float32) / np.float32(axis))).astype(np.float32)
    ang = np.concatenate([row[:, None] * inv, col[:, None] * inv], axis=-1).astype(np.float32)
    f = np.arange(P) % (HD // 2)
    sign = np.where(np.arange(P) % HD < HD // 2, -1.0, 1.0).astype(np.float32)
    return np.stack([np.cos(ang).T[f], np.sin(ang).T[f] * sign[:, None]], axis=1).astype(np.float32)


class Own:

    def __init__(self, eng, sem):
        self.eng, self.sem, self.n, self.off = eng, sem, 0, 0

    def done(self, ins):
        ins.then_inc(self.sem, 1)
        self.n += 1

    def settle(self):
        self.eng.wait_ge(self.sem, self.n + self.off)

    def enter(self, it, per):
        self.start, self.per, self.off = self.n, per, it * per

    def leave(self, count):
        assert self.n - self.start == self.per, (self.n - self.start, self.per)
        self.n, self.off = self.start + count * self.per, 0


def trunk(nc, a, out_ctx, out_lat, out_k, out_v, out_state):
    ctx = ExitStack()
    with ctx:
        base = -(-nc.sbuf_base // 64) * 64
        top = {"at": base}

        def at(name, shape, dt, offset):
            size = int(np.prod(shape[1:])) * 4
            assert offset % 32 == 0 and offset + size <= nc.sbuf_usable_end, (name, offset, size)
            return nc.alloc_sbuf_tensor_at(name, shape, dt, offset=offset)

        def area(size):
            o = top["at"]
            top["at"] += -(-size // 64) * 64
            return o

        def sem(name):
            return ctx.enter_context(nc.semaphore(name))

        def dram(name, shape):
            return nc.dram_tensor(name, shape, F32).ap()

        UB = D * 4
        raw = at("raw", [P, NRAW, D], F32, area(NRAW * UB))
        w_hi = at("w_hi", [P, NHL, D], F32R, area(NHL * UB))
        w_lo = at("w_lo", [P, NHL, D], F32R, area(NHL * UB))
        ra, rb = area(KT * N_TOK * 4), area(KT * N_TOK * 4)
        hi = at("hi", [P, KT, N_TOK], F32R, ra)
        lo = at("lo", [P, KT, N_TOK], F32R, rb)
        ident = at("ident", [P, P], F32, area(P * 4))
        mean_mat = at("mean_mat", [P, P], F32, area(P * 4))
        prm_all = at("prm_all", [P, NB, NPRM], F32, area(NB * NPRM * 4))
        misc = at("misc", [P, 32], F32, area(128))
        stats = at("stats", [P, 64], F32, area(256))
        state_col = at("state_col", [P, 2 * NB], F32, area(64))
        eps_col, lam_col, gsub_col, ones_col = (misc[:, i:i + 1] for i in range(4))
        s0 = top["at"]
        s_end = nc.sbuf_usable_end

        PLACED = {}

        def place(at0, items):
            o, made = at0, {}
            for name, shape, dt in items:
                made[name] = at(name, shape, dt, o)
                PLACED[name] = o
                o += -(-int(np.prod(shape[1:])) * 4 // 64) * 64
            assert o <= s_end, (o, s_end)
            return made

        x_in = at("x_in", [P, TT, D], F32, ra)
        xT = at("xT", [P, KT, N_TOK], F32, rb)
        A = place(s0, [("b_row", [2, D], F32), ("m_row", [2, D], F32), ("junk0", [P, D], F32),
                       ("zero", [P, D], F32), ("rows1", [48, P], F32), ("rows2", [105, P], F32),
                       ("rows3", [64, P], F32), ("cols1", [P, 48], F32), ("cols2", [P, 105], F32),
                       ("cols3", [P, 64], F32), ("sc", [P, 32], F32), ("lamv", [1, 4, 64], F32),
                       ("lamp", [1, 2, 64], F32), ("lams", [1, 8], F32), ("ones_row", [1, P], F32),
                       ("sp_a", [P, 16], F32), ("sp_b", [P, 16], F32), ("sp_c", [P, 16], F32),
                       ("sp_d", [P, 16], F32), ("A1", [P, 2, KT], F32)])
        c_hi = at("c_hi", [P, KT, 2], F32R, s0 + 50048)
        c_lo = at("c_lo", [P, KT, 2], F32R, s0 + 50048 + 128)
        assert PLACED["A1"] + 128 <= s0 + 50048
        v_stage = at("v_stage", [P, TT, 512], F32, s0)
        stage = at("stage", [P, 2, N_TOK], F32, s0 + TT * 512 * 4)
        C = place(s0, [("rope", [P, 2, N_LAT], F32), ("q", [P, N_TOK], F32), ("q_sw", [P, N_LAT], F32),
                       ("k", [P, N_TOK], F32), ("k_sw", [P, N_LAT], F32), ("k_all", [P, PAST + N_TOK], F32),
                       ("k_past", [P, P], F32), ("k_new", [P, P], F32), ("v", [P, TT + 1, P], F32),
                       ("xr", [P, N_TOK], F32), ("xc", [P, N_TOK], F32), ("gr", [P, N_TOK], F32),
                       ("rsd", [P, N_TOK], F32), ("o_n", [P, N_TOK], F32), ("lru_w", [P, 4, P], F32),
                       ("prm", [P, 16], F32), ("att", [P, 32], F32), ("g_stage", [P, 2, N_TOK], F32),
                       ("probs", [P, 2, 2, N_TOK], F32), ("pT", [P, TT, N_LAT], F32), ("pT_ctx", [P, P], F32)])
        reg1 = PLACED["probs"]
        L = place(reg1, [(n, [P, N_TOK], F32) for n in
                         ("lr", "li", "la", "lt", "ld", "h_f", "h_b", "gel")])
        mix = at("mix", [P, KT, N_TOK], F32, s0)
        G = place(s0 + KT * N_TOK * 4, [("gate", [P, 2, 2, N_TOK], F32), ("mix_b", [P, N_TOK], F32)])
        t_out = at("t_out", [P, TT, D], F32, s0)
        R1 = place(ra, [("G1", [P, D], F32), ("A2", [P, D], F32), ("B2", [P, D], F32), ("x_t", [P, 2, D], F32)])
        R2 = place(rb, [("h2", [P, 2, D], F32), ("h2T", [P, KT, P], F32), ("junk1", [P, D], F32),
                        ("row_t", [P, D], F32)])
        T = place(s0 + TT * D * 4, [("aff", [P, 16], F32), ("affT", [NE, N_TOK], F32), ("vals", [NE, CAP], F32),
                                    ("idx", [NE, CAP], U32), ("idx_f", [NE, CAP], F32), ("wr", [P, KT, NE], F32),
                                    ("sm", [P, 8], F32), ("sidx", [P, 1], U32),
                                    ("val_t", [P, NE + 1], F32), ("idx_t", [P, NE + 1], U32),
                                    ("val_e", [P, 1], F32), ("idx_e", [P, 1], U32)])
        E = place(ra, [("xs", [P, D], F32), ("ye", [P, D], F32), ("hid", [P, D_EXP], F32), ("junk_e", [P, D_EXP], F32)])
        xs_hi = at("xs_hi", [P, KT, CAP], F32R, ra + 24576)
        xs_lo = at("xs_lo", [P, KT, CAP], F32R, ra + 24576 + 5120)
        hid_hi = at("hid_hi", [P, 8, CAP], F32R, ra + 24576 + 10240)
        hid_lo = at("hid_lo", [P, 8, CAP], F32R, ra + 24576 + 12800)
        Z = place(rb, [("G2", [P, 2, D], F32), ("f_t", [P, D], F32), ("x2_t", [P, D], F32), ("junk2", [P, D], F32)])
        state_rows = at("state_rows", [2 * NB, P], F32, s0)
        ps = ctx.enter_context(nc.psum_tensor("ps", [P, 8, 512], F32))

        d_mod = dram("d_mod", [2, 6 * D])
        d_proj = dram("d_proj", [72 * P, N_TOK])
        d_v = dram("d_v", [N_TOK, D_RNN])
        d_z = dram("d_z", [KT * P, N_TOK])
        d_x2 = dram("d_x2", [N_TOK, D])
        d_h2 = dram("d_h2", [N_TOK, D])
        d_f = dram("d_f", [N_TOK, D])

        raw_loaded = [sem(f"raw_loaded{i}") for i in range(NRAW)]
        hi_ready = sem("hi_ready")
        lo_ready = sem("lo_ready")
        units_used = sem("units_used")
        phase = sem("phase")
        pool_own, dve_own, act_own = sem("pool_own"), sem("dve_own"), sem("act_own")
        par_loaded, x_lat_loaded, x_ctx_loaded = sem("par_loaded"), sem("x_lat_loaded"), sem("x_ctx_loaded")
        zero_set = sem("zero_set")
        S = {n: sem(n) for n in (
            "const_set", "rows_turned", "cols_ready", "c_act", "c_ready", "lam_prod", "lam_exp", "lam_val", "lam_spread",
            "sqrt_x", "xn_ready", "x_turned", "xt_act", "xt_dve", "b_loaded", "m_row_ready", "m_stored",
            "zero_stored", "rows3_loaded", "rows3_turned", "a1_ready", "tok_hi", "tok_lo", "sp_abs", "sp_exp",
            "bank_done", "bank_taken", "v_stored", "in_a_done", "in_taken", "in_stored",
            "rope_loaded", "xr_loaded", "lruw_loaded", "gr_loaded", "q_loaded", "k_loaded", "kv_loaded", "prm_set",
            "xc_ready", "rope_done", "kt_done", "kt_taken", "knew_stored", "gate_a_done", "gate_taken",
            "gate_stored", "lru_mm", "lru_sig", "lru_at", "lru_q", "lru_sqrt", "lru_b", "lru_scan",
            "gelu_done", "y_ready", "y_stored", "score_done", "score_max", "score_exp", "pd_ready", "pdT_done",
            "pdT_taken", "av_done", "o_sq", "ms_done", "ms_sqrt", "o_ready", "o_stored",
            "z_loaded", "z_hi", "z_lo", "g_loaded0", "g_loaded1", "g_sig", "ab_a", "mix_done", "mix_hi", "mix_lo",
            "o_taken", "rs1_sum", "rs1_sqrt",
            "vec_loaded", "vec_ready", "xt_loaded0", "xt_loaded1", "x2_ready", "x2_sqrt", "h2_ready", "x2_stored",
            "h2_stored", "h2T_done", "h2T_taken", "logit_done", "logit_max", "logit_exp", "aff_ready", "affT_done",
            "affT_taken", "top_ready", "topT_done", "wr_loaded",
            "idx_ready", "gathered", "xsT_done", "xs_hi_done", "xs_lo_done", "silu_done", "hid_done", "hidT_done",
            "hidT_hi", "hidT_lo", "val_set", "ye_act", "ye_dve", "scattered", "g2_loaded", "g2_ready",
            "f_loaded", "x2_loaded", "f_sqrt", "y_done", "y_out", "passed", "m_row_free", "v_free", "stage_free", "g_stage_free", "k_new_free", "o_n_free", "ye_free", "state_turned", "state_row", "state_stored")}

        CREDIT = {"m_row_ready": 1, "m_row_free": 1, "bank_taken": TT, "v_free": 1, "in_taken": 2, "stage_free": 2,
                  "gate_taken": 2, "g_stage_free": 2, "k_new_free": 1, "o_ready": 1, "o_n_free": 1, "pdT_taken": 1,
                  "mix_done": 2, "o_taken": TT, "ye_act": 1, "ye_dve": 1, "ye_free": 1}

        def give(eng, *names):
            for n in names:
                eng.sem_inc(S[n], CREDIT[n])

        def wait(eng, name, value):
            eng.wait_ge(S[name], value + CREDIT.get(name, 0))

        def raw_wait(eng, slot, quad):
            eng.wait_ge(raw_loaded[slot], (quad + 1) * INC)

        def split_hi(act, quad, j):
            quad, j = quad + j // NRAW, j % NRAW
            raw_wait(act, j, quad)
            act.wait_ge(units_used, quad * NRAW + j + 1)
            act.activation(w_hi[:, j % NHL, :], raw[:, j, :], ACT.Copy).then_inc(hi_ready, 1)

        def split_lo(dve, quad, j):
            quad, j = quad + j // NRAW, j % NRAW
            dve.wait_ge(hi_ready, quad * NRAW + j + 1)
            dve.tensor_tensor(w_lo[:, j % NHL, :], raw[:, j, :], w_hi[:, j % NHL, :].bitcast(F32),
                              ALU.subtract).then_inc(lo_ready, 1)

        def unit_wait(pe, quad, j):
            pe.wait_ge(lo_ready, NRAW + quad * NRAW + j + 1)

        def change(eng, k):
            eng.drain().then_inc(phase, 1)
            eng.wait_ge(phase, 4 * k)

        def o_bank_wait(eng, c, t):
            if t < TT - 1:
                eng.wait_ge(S["bank_done"], 2 * (TT - 1) + c * (TT - 1) + t + 1)
            else:
                eng.wait_ge(units_used, (Q_O + c + 1) * 4 + NHL)

        def halves(tile):
            return tile.rearrange("p (a n) -> p a n", a=2)

        def three(pe, out, s_hi, s_lo, m_hi, m_lo, start, stop):
            pe.matmul(out, s_lo, m_hi, start=start, stop=False)
            pe.matmul(out, s_hi, m_lo, start=False, stop=False)
            return pe.matmul(out, s_hi, m_hi, start=False, stop=stop)

        block = ctx.enter_context(nc.Block())

        @block.sync
        def _(sp):
            def load(quad, j, parts):
                sp.wait_ge(lo_ready, quad * NRAW + j + 1)
                for dst, src in parts:
                    sp.dma_start(dst, src).then_inc(raw_loaded[j], INC // 2)

            def rows(w, k, c0):
                return [(slice(0, 1024), w[bass.ds(k * P, P), bass.ds(c0, 1024)]),
                        (slice(1024, 2048), w[bass.ds(k * P, P), bass.ds(c0 + 1024, 1024)])]

            w_mod, w_in = a["w_mod"][0], a["w_in"][0]
            with sp.Fori(0, 6) as g:
                for k in range(KT):
                    load(Q_MOD + g * 4 + k // NRAW, k % NRAW,
                         [(raw[:, k % NRAW, s], src) for s, src in rows(w_mod, k, g * D)])

            def wide(w, j, kq, c0):
                v = raw[:, j, :].rearrange("p (k n) -> p k n", k=4)
                return [(v[:, 2 * i:2 * i + 2, :],
                         w[(4 * kq + 2 * i) * P:(4 * kq + 2 * i + 2) * P, bass.ds(c0, 512)].rearrange(
                             "(k p) n -> p k n", p=P)) for i in range(2)]

            def tall(pieces, j, c0):
                v = raw[:, j, :].rearrange("p (k n) -> p k n", k=KT)
                return [(v[:, 8 * i:8 * i + 8, :], w[:, bass.ds(c0, P)].rearrange("(k p) n -> p k n", p=P))
                        for i, w in enumerate(pieces)]

            with sp.Fori(0, 2) as c:
                for kq in range(4):
                    load(Q_V + c, kq, wide(w_in, kq, kq, V_COL + c * 512))
            w_in2 = [w_in[0:D // 2], w_in[D // 2:D]]
            with sp.Fori(0, 8) as i:
                for j in range(4):
                    load(Q_IN + i, j, tall(w_in2, j, (i * 4 + j) * P))
            with sp.Fori(0, 8) as i:
                for j in range(4):
                    load(Q_GATE + i, j, tall(w_in2, j, GATE_COL + (i * 4 + j) * P))
            with sp.Fori(0, 4) as i:
                for j in range(4):
                    load(Q_AB + i, j, tall([a["w_a_out"][0], a["w_b_out"][0]], j, (i * 4 + j) * P))
            with sp.Fori(0, 4) as c:
                for kq in range(4):
                    load(Q_O + c, kq, wide(a["w_o"][0], kq, kq, c * 512))
            wg = a["w_e_gate"][0].rearrange("e k f -> (e k) f")
            wu = a["w_e_up"][0].rearrange("e k f -> (e k) f")
            wd = a["w_e_down"][0].rearrange("e k f -> (e k) f")
            with sp.Fori(0, NE) as e:
                for k in range(KT):
                    load(Q_EXP + e * 6 + k // 4, k % 4,
                         [(raw[:, k % 4, 0:1024], wg[bass.ds(e * D + k * P, P), :]),
                          (raw[:, k % 4, 1024:2048], wu[bass.ds(e * D + k * P, P), :])])
                for k in range(8):
                    load(Q_EXP + e * 6 + 4 + k // 4, k % 4,
                         [(raw[:, k % 4, s * 1024:(s + 1) * 1024],
                           wd[bass.ds(e * D_EXP + k * P, P), s * 1024:(s + 1) * 1024]) for s in range(2)])

        @block.gpsimd
        def _(pool):
            give(pool, "m_row_free", "v_free", "stage_free", "g_stage_free", "k_new_free", "o_n_free", "ye_free")

            def plain():
                pool.sem_inc(S["passed"], 1)

            def stored(done, value, free):
                pool.wait_ge(S[done], value)
                pool.sem_inc(S[free], 1)

            def flat(x):
                return x.rearrange("(r p) -> r p", p=P)

            def heads(x):
                return x.rearrange("t h e -> t (h e)")

            r1, r2 = A["rows1"], A["rows2"]
            loads = [(ident[:], a["ident"]), (r1[0:16, :], flat(a["c"][0])), (r1[16:32, :], flat(a["c_ctx"])),
                     (r1[32:48, :], flat(a["g_pre1"][0])),
                     (r2[0:32, :], a["conv_w"][0].rearrange("t (b p) -> (t b) p", p=P)),
                     (r2[32:40, :], flat(a["conv_b"][0])),
                     (r2[40:56, :], a["lru_br"][0].rearrange("d (b p) -> (d b) p", p=P)),
                     (r2[56:72, :], a["lru_bi"][0].rearrange("d (b p) -> (d b) p", p=P)),
                     (r2[72:88, :], a["lru_lam"][0].rearrange("d (b p) -> (d b) p", p=P)),
                     (r2[88:104, :], a["state_rnn"][0, 0].rearrange("d (b p) -> (d b) p", p=P)),
                     (r2[104:105, :], a["g_sub"])]
            loads += [(A["lamv"][0:1, i, :], a[n]) for i, n in enumerate(("lam_q1", "lam_q2", "lam_k1", "lam_k2"))]
            assert len(loads) == N_PAR
            for dst, src in loads:
                pool.dma_start(dst, src).then_inc(par_loaded, 16)
            pool.memset(A["zero"][:], 0.0).then_inc(zero_set, 1)
            pool.wait_ge(zero_set, 1)
            for t in range(TT):
                pool.dma_start(d_f[t * P:(t + 1) * P, :], A["zero"][:]).then_inc(S["zero_stored"], 16)
            with pool.Fori(0, 6) as g:
                wait(pool, "m_row_ready", g)
                plain()
                pool.dma_start(A["b_row"][:], a["b_mod"][0:1, bass.ds(g * D, D)].to_broadcast([2, D])
                               ).then_inc(S["b_loaded"], 16)
                wait(pool, "m_row_ready", g + 1)
                plain()
                pool.dma_start(d_mod[:, bass.ds(g * D, D)], A["m_row"][:]).then_inc(S["m_stored"], 16)
                stored("m_stored", (g + 1) * 16, "m_row_free")
            for i, (r, g) in enumerate(((0, 0), (0, 1), (1, 0), (1, 1))):
                pool.dma_start(A["rows3"][16 * i:16 * i + 16, :], flat(d_mod[r, g * D:(g + 1) * D])
                               ).then_inc(S["rows3_loaded"], 16)
            pool.wait_ge(S["zero_stored"], TT * 16)
            change(pool, 1)

            with pool.Fori(0, 2) as c:
                wait(pool, "bank_taken", TT * (c + 1))
                plain()
                pool.dma_start(d_v[:, bass.ds(c * 512, 512)].rearrange("(t p) n -> p t n", p=P), v_stage[:]
                               ).then_inc(S["v_stored"], 16)
                pool.dma_start(heads(out_v[0, 0])[:, bass.ds(c * 512, 512)], v_stage[:, TT - 1, :]
                               ).then_inc(S["v_stored"], 16)
                stored("v_stored", c * 32 + 32, "v_free")
            with pool.Fori(0, 8) as i:
                for j in range(4):
                    wait(pool, "in_taken", 2 * (i * 4 + j + 1))
                    plain()
                    pool.dma_start(d_proj[bass.ds((i * 4 + j) * P, P), :], stage[:, j % 2, :]
                                   ).then_inc(S["in_stored"], 16)
                    stored("in_stored", (i * 4 + j + 1) * 16, "stage_free")
            change(pool, 2)

            pool.dma_start(C["rope"][:], a["rope"]).then_inc(S["rope_loaded"], 16)
            with pool.Fori(0, NH) as h:
                def tile_of(n):
                    return d_proj[bass.ds((h + n) * P, P), :]

                pool.dma_start(C["xr"][:], tile_of(0)).then_inc(S["xr_loaded"], 16)
                for i, (w, d) in enumerate((("lru_wr", 0), ("lru_wi", 0), ("lru_wr", 1), ("lru_wi", 1))):
                    pool.dma_start(C["lru_w"][:, i, :], a[w][0, d].rearrange("b i j -> (b i) j")[bass.ds(h * P, P), :]
                                   ).then_inc(S["lruw_loaded"], 16)
                pool.dma_start(C["k_past"][:], heads(a["cache_k"][0, 0])[:, bass.ds(h * P, P)]
                               ).then_inc(S["kv_loaded"], 16)
                pool.dma_start(C["v"][:, 0, :], heads(a["cache_v"][0, 0])[:, bass.ds(h * P, P)]
                               ).then_inc(S["kv_loaded"], 16)
                pool.dma_start(C["v"][:, 1:TT + 1, :], d_v[:, bass.ds(h * P, P)].rearrange("(t p) n -> p t n", p=P)
                               ).then_inc(S["kv_loaded"], 16)
                for name, swapped, n, ready in (("k", "k_sw", 24, "k_loaded"), ("q", "q_sw", 16, "q_loaded")):
                    pool.dma_start(C[name][:], tile_of(n)).then_inc(S[ready], 16)
                    for s in range(4):
                        pool.dma_start(C[swapped][32 * s:32 * s + 32, :],
                                       d_proj[bass.ds((h + n) * P + 32 * (s ^ 1), 32), 0:N_LAT]
                                       ).then_inc(S[ready], 16)
                pool.dma_start(C["gr"][:], tile_of(8)).then_inc(S["gr_loaded"], 16)

                def store_gate(j):
                    wait(pool, "gate_taken", 2 * (h * 4 + j) + 2)
                    plain()
                    pool.dma_start(d_proj[bass.ds((h * 4 + 40 + j) * P, P), :], C["g_stage"][:, j % 2, :]
                                   ).then_inc(S["gate_stored"], 16)
                    stored("gate_stored", (h * 4 + j + 1) * 16, "g_stage_free")

                pool.wait_ge(S["kt_taken"], 2 * h + 2)
                plain()
                pool.dma_start(heads(out_k[0, 0])[:, bass.ds(h * P, P)], C["k_new"][:]
                               ).then_inc(S["knew_stored"], 16)
                stored("knew_stored", h * 16 + 16, "k_new_free")
                store_gate(0)
                pool.wait_ge(S["y_ready"], h + 1)
                plain()
                pool.dma_start(d_z[bass.ds(h * P, P), :], L["h_f"][:]).then_inc(S["y_stored"], 16)
                store_gate(1)
                store_gate(2)
                store_gate(3)
                wait(pool, "o_ready", 2 * h + 2)
                plain()
                pool.dma_start(d_z[bass.ds((h + 8) * P, P), :], C["o_n"][:]).then_inc(S["o_stored"], 16)
                stored("o_stored", h * 16 + 16, "o_n_free")
            pool.wait_ge(S["y_stored"], NH * 16)
            change(pool, 3)

            zs = d_z.rearrange("(k p) n -> p k n", p=P)
            for q in range(4):
                pool.dma_start(mix[:, 4 * q:4 * q + 4, :], zs[:, 4 * q:4 * q + 4, :]).then_inc(S["z_loaded"], 16)
                pool.wait_ge(S["z_loaded"], 16 * (q + 1))
            with pool.Fori(0, 4) as i:
                for j in range(4):
                    wait(pool, "mix_done", i * 4 + j - 1)
                    plain()
                    for s in range(2):
                        pool.dma_start(G["gate"][:, j % 2, s, :], d_proj[bass.ds((i * 4 + 40 + s * KT + j) * P, P), :]
                                       ).then_inc(S[f"g_loaded{j % 2}"], 16)
            change(pool, 4)
            change(pool, 5)

            def mod_row(r, g):
                return d_mod[r:r + 1, g * D:(g + 1) * D].to_broadcast([P, D])

            def store_tile(t):
                pool.wait_ge(S["x2_ready"], t + 1)
                pool.dma_start(d_x2[t * P:(t + 1) * P, :], t_out[:, t, :]).then_inc(S["x2_stored"], 16)
                pool.wait_ge(S["h2_ready"], t + 1)
                pool.dma_start(d_h2[t * P:(t + 1) * P, :], R2["h2"][:, t % 2, :]).then_inc(S["h2_stored"], 16)

            gp1, gp2 = (a[n][0:1, :].to_broadcast([P, D]) for n in ("g_post1", "g_pre2"))
            for t in range(TT):
                if t in (0, TT - 1):
                    r = int(t > 0)
                    if t:
                        pool.wait_ge(S["h2_ready"], t)
                    for dst, src in ((R1["G1"], mod_row(r, 2)), (R2["row_t"], gp1), (R1["A2"], mod_row(r, 4)),
                                     (R1["B2"], mod_row(r, 3))):
                        pool.dma_start(dst[:], src).then_inc(S["vec_loaded"], 16)
                    if t == 0:
                        pool.dma_start(R1["x_t"][:, 0, :], a["x_sample"][0][0:P, :]).then_inc(S["xt_loaded0"], 16)
                        pool.dma_start(T["wr"][:], a["w_router"][0].rearrange("(k p) e -> p k e", p=P)
                                       ).then_inc(S["wr_loaded"], 16)
                    pool.wait_ge(S["vec_ready"], 2 * r + 1)
                    pool.dma_start(R2["row_t"][:], gp2).then_inc(S["vec_loaded"], 16)
                if t >= 1:
                    if t >= 2:
                        pool.wait_ge(S["x2_ready"], t - 1)
                    src = a["x_sample"][0][t * P:(t + 1) * P, :] if t < TT - 1 else a["x_prompt"][0]
                    pool.dma_start(R1["x_t"][:, t % 2, :], src).then_inc(S[f"xt_loaded{t % 2}"], 16)
                    store_tile(t - 1)
            store_tile(TT - 1)
            pool.wait_ge(S["x2_stored"], TT * 16)
            pool.wait_ge(S["h2_stored"], TT * 16)
            change(pool, 6)

            def gather(e):
                pool.wait_ge(S["idx_ready"], e + 1)
                plain()
                pool.indirect_dma_start(E["xs"][0:CAP, :], None, d_h2,
                                        bass.IndirectOffsetOnAxis(T["idx_e"][0:CAP, 0:1], 0)
                                        ).then_inc(S["gathered"], 16)

            def scatter(e):
                wait(pool, "ye_act", e + 1)
                wait(pool, "ye_dve", e + 1)
                plain()
                pool.indirect_dma_start(d_f, bass.IndirectOffsetOnAxis(T["sidx"][0:CAP, 0:1], 0), E["ye"][0:CAP, :],
                                        None, compute_op=ALU.add).then_inc(S["scattered"], 16)
                stored("scattered", (e + 1) * 16, "ye_free")

            gather(0)
            for r in range(2):
                pool.dma_start(Z["G2"][:, r, :], mod_row(r, 5)).then_inc(S["g2_loaded"], 16)
            pool.dma_start(Z["f_t"][:], a["g_post2"][0:1, :].to_broadcast([P, D])).then_inc(S["g2_loaded"], 16)
            with pool.Fori(0, NE - 1) as e:
                gather(e + 1)
                scatter(e)
            scatter(NE - 1)
            change(pool, 7)

        @block.scalar
        def _(act):
            give(act, "in_taken", "gate_taken", "pdT_taken", "ye_act")
            own = Own(act, act_own)
            act.dma_start(x_in[:, 0:TT - 1, :], a["x_sample"][0].rearrange("(t p) d -> p t d", p=P)
                          ).then_inc(x_lat_loaded, 16)
            act.dma_start(x_in[:, TT - 1, :], a["x_prompt"][0]).then_inc(x_ctx_loaded, 16)
            act.wait_ge(S["cols_ready"], 1)
            act.activation(A["sc"][:], A["cols1"][:, 0:32], ACT.Silu).then_inc(S["c_act"], 1)
            act.wait_ge(S["c_act"], 1)
            act.activation(c_hi[:], A["sc"][:].rearrange("p (v k) -> p k v", v=2), ACT.Copy).then_inc(S["c_act"], 1)
            act.wait_ge(S["lam_prod"], 1)
            act.activation(A["lams"][0:1, 2:4], A["lams"][0:1, 0:2], ACT.Exp).then_inc(S["lam_exp"], 1)
            act.wait_ge(S["sp_abs"], 1)
            act.activation(A["sp_b"][:], A["sp_a"][:], ACT.Exp, scale=-1.0).then_inc(S["sp_exp"], 1)
            split_hi(act, Q_MOD, 0)
            for t in range(TT):
                if t == 0:
                    act.wait_ge(x_lat_loaded, 16)
                if t == TT - 1:
                    act.wait_ge(x_ctx_loaded, 16)
                if t:
                    own.settle()
                own.done(act.activation(A["junk0"][:], x_in[:, t, :], ACT.Square, accum_out=stats[:, t:t + 1]))
            act.wait_ge(S["const_set"], 1)
            own.settle()
            act.activation(stats[:, 8:8 + TT], stats[:, 0:TT], ACT.Sqrt, bias=eps_col, scale=1.0 / D
                           ).then_inc(S["sqrt_x"], 1)
            for g in range(0, 4 * TT, 2):
                act.wait_ge(S["x_turned"], g + 1)
                t, kq = g // 4, g % 4
                act.activation(xT[:, 4 * kq:4 * kq + 4, t * P:(t + 1) * P],
                               ps[:, 4 + kq, :].rearrange("p (k n) -> p k n", k=4), ACT.Copy).then_inc(S["xt_act"], 1)
            with act.Fori(0, 6) as g:
                for k in range(KT):
                    split_hi(act, Q_MOD + g * 4, k + 1)
            act.wait_ge(S["a1_ready"], 1)
            for k in range(KT):
                for r, s in ((0, slice(0, N_LAT)), (1, slice(N_LAT, N_TOK))):
                    last = act.activation(hi[:, k, s], xT[:, k, s], ACT.Identity, scale=A["A1"][:, r, k:k + 1],
                                          bias=A["cols3"][:, 32 * r + k:32 * r + k + 1])
                last.then_inc(S["tok_hi"], 1)
            change(act, 1)

            with act.Fori(0, 2) as c:
                for kq in range(4):
                    split_hi(act, Q_V + c, kq + 1)
            with act.Fori(0, 8) as i:
                for j in range(4):
                    split_hi(act, Q_IN + i, j + 1)
                    act.wait_ge(S["in_a_done"], i * 4 + j + 1)
                    wait(act, "stage_free", i * 4 + j - 1)
                    act.activation(stage[:, j % 2, 0:HALF], ps[:, 5, 0:HALF], ACT.Copy).then_inc(S["in_taken"], 1)
                    act.wait_ge(units_used, i * 4 + j + Q_IN * 4 + 1 + NHL)
                    act.activation(stage[:, j % 2, HALF:N_TOK], ps[:, 6, 0:HALF], ACT.Copy
                                   ).then_inc(S["in_taken"], 1)
            change(act, 2)

            att = C["att"]
            with act.Fori(0, NH) as h:
                def take(j, half):
                    if half == 0:
                        act.wait_ge(S["gate_a_done"], h * 4 + j + 1)
                        wait(act, "g_stage_free", h * 4 + j - 1)
                    else:
                        act.wait_ge(units_used, h * 4 + Q_GATE * 4 + j + 1 + NHL)
                    act.activation(C["g_stage"][:, j % 2, half * HALF:(half + 1) * HALF], ps[:, 5 + half, 0:HALF],
                                   ACT.Copy).then_inc(S["gate_taken"], 1)

                def lru_gates(d):
                    act.wait_ge(S["lru_mm"], h * 2 + d + 1)
                    if d:
                        act.wait_ge(S["lru_b"], h * 2 + d)
                    for i, dst in ((0, "lr"), (1, "li")):
                        act.activation(halves(L[dst][:]), ps[:, 2 * i:2 * i + 2, 0:HALF], ACT.Sigmoid,
                                       bias=C["prm"][:, (BR, BI)[i] + d:(BR, BI)[i] + d + 1]).then_inc(S["lru_sig"], 1)
                    if d:
                        act.wait_ge(S["lru_scan"], h * 2 + d)
                    act.wait_ge(S["lru_sig"], h * 4 + 2 * d + 2)
                    act.activation(L["la"][:], L["lr"][:], ACT.Exp, scale=C["prm"][:, NEG + d:NEG + d + 1]
                                   ).then_inc(S["lru_at"], 1)
                    act.activation(L["lt"][:], L["lr"][:], ACT.Tanh, scale=C["prm"][:, LAM_ + d:LAM_ + d + 1]
                                   ).then_inc(S["lru_at"], 1)

                def lru_root(d):
                    act.wait_ge(S["lru_q"], h * 2 + d + 1)
                    act.activation(L["lt"][:], L["lt"][:], ACT.Sqrt, scale=2.0).then_inc(S["lru_sqrt"], 1)

                def exps(qt):
                    act.wait_ge(S["score_max"], h * TT + qt + 1)
                    if qt == 0:
                        act.wait_ge(S["y_ready"], h + 1)
                    if qt >= 2:
                        act.wait_ge(S["pdT_done"], h * TT + qt - 1)
                    for c in range(2):
                        if qt < TT - 1:
                            dst, src = halves(C["probs"][:, qt % 2, c, :]), ps[:, 2 * c:2 * c + 2, 0:HALF]
                        else:
                            dst, src = C["probs"][:, qt % 2, c, 0:P], ps[:, 2 * c, 0:P]
                        i = 4 * (qt % 2) + c
                        act.activation(dst, src, ACT.Exp, scale=ATT_SCALE, bias=att[:, i:i + 1],
                                       accum_out=att[:, 8 + i:9 + i]).then_inc(S["score_exp"], 1)

                def take_T(qt):
                    act.wait_ge(S["pdT_done"], h * TT + qt + 1)
                    if qt == 0:
                        act.wait_ge(S["y_stored"], h * 16 + 16)
                    if qt < TT - 1:
                        act.activation(C["pT"][:, 0:4, qt * P:(qt + 1) * P],
                                       ps[:, 4, :].rearrange("p (k n) -> p k n", k=4), ACT.Copy)
                        act.activation(C["pT"][:, 4, qt * P:(qt + 1) * P], ps[:, 7, 0:P], ACT.Copy
                                       ).then_inc(S["pdT_taken"], 1)
                    else:
                        act.activation(C["pT_ctx"][:], ps[:, 4, 0:P], ACT.Copy).then_inc(S["pdT_taken"], 1)

                split_hi(act, Q_GATE + h, 1)
                act.wait_ge(S["prm_set"], h + 1)
                take(0, 0)
                lru_gates(0)
                take(0, 1)
                lru_root(0)
                split_hi(act, Q_GATE + h, 2)
                lru_gates(1)
                take(1, 0)
                lru_root(1)
                act.wait_ge(S["gr_loaded"], h * 16 + 16)
                act.activation(L["gel"][:], C["gr"][:], ACT.Gelu_apprx_tanh).then_inc(S["gelu_done"], 1)
                exps(0)
                take(1, 1)
                split_hi(act, Q_GATE + h, 3)
                exps(1)
                take_T(0)
                exps(2)
                take(2, 0)
                take_T(1)
                exps(3)
                take_T(2)
                exps(4)
                take(2, 1)
                take_T(3)
                split_hi(act, Q_GATE + h, 4)
                take_T(4)
                take(3, 0)
                act.wait_ge(S["av_done"], h + 1)
                for b, s in ((0, slice(0, N_LAT)), (1, slice(N_LAT, N_TOK))):
                    last = act.activation(C["probs"][:, 0, 0, s], ps[:, b, 0:s.stop - s.start], ACT.Square)
                last.then_inc(S["o_sq"], 1)
                act.wait_ge(S["ms_done"], h + 1)
                for b, s in ((2, slice(0, N_LAT)), (3, slice(N_LAT, N_TOK))):
                    last = act.activation(C["rsd"][:, s], ps[:, b, 0:s.stop - s.start], ACT.Sqrt, bias=eps_col)
                last.then_inc(S["ms_sqrt"], 1)
                take(3, 1)
            change(act, 3)

            for k in range(KT):
                if k % 4 == 0:
                    act.wait_ge(S["z_loaded"], 16 * (k // 4 + 1))
                act.activation(hi[:, k, :], mix[:, k, :], ACT.Copy).then_inc(S["z_hi"], 1)
            with act.Fori(0, 4) as i:
                for j in range(4):
                    act.wait_ge(S[f"g_loaded{j % 2}"], (i * 2 + j // 2) * 32 + 32)
                    act.activation(G["gate"][:, j % 2, :, :], G["gate"][:, j % 2, :, :], ACT.Sigmoid
                                   ).then_inc(S["g_sig"], 1)
                    split_hi(act, Q_AB + i, j + 1)
            change(act, 4)

            for k in range(KT):
                act.activation(hi[:, k, :], mix[:, k, :], ACT.Copy).then_inc(S["mix_hi"], 1)
            for c in range(4):
                for kq in range(4):
                    split_hi(act, Q_O + c, kq + 1)
                for t in range(TT):
                    wait(act, "o_taken", c * TT + t + 1)
                    own.settle()
                    own.done(act.activation(G["mix_b"][:, 0:512], t_out[:, t, c * 512:(c + 1) * 512], ACT.Square,
                                            accum_out=stats[:, 16 + 4 * t + c:17 + 4 * t + c]))
            change(act, 5)

            act.wait_ge(S["rs1_sum"], 1)
            act.activation(stats[:, 40:40 + TT], stats[:, 40:40 + TT], ACT.Sqrt, bias=eps_col, scale=1.0 / D
                           ).then_inc(S["rs1_sqrt"], 1)
            for t in range(TT):
                act.wait_ge(S["x2_ready"], t + 1)
                own.done(act.activation(R2["junk1"][:], t_out[:, t, :], ACT.Square, accum_out=stats[:, 48 + t:49 + t]))
                own.settle()
                act.activation(stats[:, 48 + t:49 + t], stats[:, 48 + t:49 + t], ACT.Sqrt, bias=eps_col, scale=1.0 / D
                               ).then_inc(S["x2_sqrt"], 1)
                act.wait_ge(S["h2T_done"], t + 1)
                act.activation(R2["h2T"][:].rearrange("p (b k) n -> p b (k n)", b=4), ps[:, 0:4, :], ACT.Copy
                               ).then_inc(S["h2T_taken"], 1)
                act.wait_ge(S["logit_max"], t + 1)
                act.activation(T["aff"][:], ps[:, 4, 0:NE], ACT.Exp, bias=T["sm"][:, 1:2], accum_out=T["sm"][:, 2:3]
                               ).then_inc(S["logit_exp"], 1)
            change(act, 6)

            def take_xs(e):
                act.wait_ge(S["xsT_done"], e + 1)
                act.activation(xs_hi[:].rearrange("p (b k) n -> p b (k n)", b=4), ps[:, 0:4, 0:4 * CAP], ACT.Copy
                               ).then_inc(S["xs_hi_done"], 1)

            def expert(e, last):
                quad = Q_EXP + e * 6
                for k in range(KT):
                    split_hi(act, quad, k + 1)
                act.wait_ge(units_used, (quad + 4) * 4 + NHL)
                act.activation(E["hid"][0:CAP, :].rearrange("p (b n) -> p b n", b=2), ps[0:CAP, 0:2, :], ACT.Silu
                               ).then_inc(S["silu_done"], 1)
                act.wait_ge(S["hidT_done"], e + 1)
                act.activation(hid_hi[:].rearrange("p (b k) n -> p b (k n)", b=2), ps[:, 4:6, 0:4 * CAP], ACT.Copy
                               ).then_inc(S["hidT_hi"], 1)
                for k in range(8):
                    if not (last and k == 7):
                        split_hi(act, quad, KT + k + 1)
                    if k == 2 and not last:
                        take_xs(e + 1)
                act.wait_ge(units_used, (quad + 6) * 4 + NHL)
                act.wait_ge(S["val_set"], e + 1)
                act.activation(E["ye"][0:CAP, 0:1024].rearrange("p (b n) -> p b n", b=2), ps[0:CAP, 4:6, :],
                               ACT.Identity, scale=T["val_e"][0:CAP, :]).then_inc(S["ye_act"], 1)

            take_xs(0)
            with act.Fori(0, NE - 1) as e:
                expert(e, False)
            expert(NE - 1, True)
            change(act, 7)

            for t in range(TT):
                if t:
                    act.wait_ge(S["y_out"], t * 16)
                act.dma_start(Z["f_t"][:], d_f[t * P:(t + 1) * P, :]).then_inc(S["f_loaded"], 16)
                act.dma_start(Z["x2_t"][:], d_x2[t * P:(t + 1) * P, :]).then_inc(S["x2_loaded"], 16)
                act.wait_ge(S["f_loaded"], (t + 1) * 16)
                own.done(act.activation(Z["junk2"][:], Z["f_t"][:], ACT.Square, accum_out=stats[:, 0:1]))
                own.settle()
                act.activation(stats[:, 1:2], stats[:, 0:1], ACT.Sqrt, bias=eps_col, scale=1.0 / D
                               ).then_inc(S["f_sqrt"], 1)
                act.wait_ge(S["y_done"], t + 1)
                dst = out_lat[0, t * P:(t + 1) * P, :] if t < TT - 1 else out_ctx[0]
                act.dma_start(dst, Z["f_t"][:]).then_inc(S["y_out"], 16)
            act.wait_ge(S["state_row"], 1)
            act.dma_start(out_state[0, 0].rearrange("d (b p) -> (d b) p", p=P), state_rows[:]
                          ).then_inc(S["state_stored"], 16)
            act.wait_ge(S["y_out"], TT * 16)
            act.wait_ge(S["state_stored"], 16)

        @block.vector
        def _(dve):
            give(dve, "m_row_ready", "bank_taken", "o_ready", "mix_done", "o_taken", "ye_dve")
            dve.sem_inc(lo_ready, NRAW)
            own = Own(dve, dve_own)
            TS, TTn, STT = dve.tensor_scalar, dve.tensor_tensor, dve.scalar_tensor_tensor

            dve.memset(eps_col, EPS)
            dve.memset(mean_mat[:], 1.0 / P)
            dve.memset(A["ones_row"][:], 1.0).then_inc(S["const_set"], 1)
            dve.wait_ge(S["rows_turned"], 2)
            dve.tensor_copy(A["cols1"][:], ps[:, 7, 0:48]).then_inc(S["cols_ready"], 1)
            dve.tensor_copy(A["cols2"][:], ps[:, 7, 128:233]).then_inc(S["cols_ready"], 1)
            dve.wait_ge(S["c_act"], 2)
            TTn(c_lo[:], A["sc"][:].rearrange("p (v k) -> p k v", v=2), c_hi[:].bitcast(F32), ALU.subtract
                ).then_inc(S["c_ready"], 1)
            dve.wait_ge(par_loaded, N_PAR * 16)
            own.done(TTn(A["lamp"][:], A["lamv"][:, 0:2, :], A["lamv"][:, 2:4, :], ALU.mult))
            own.settle()
            dve.tensor_reduce(A["lams"][0:1, 0:2], A["lamp"][:], AX.X, ALU.add).then_inc(S["lam_prod"], 1)
            dve.wait_ge(S["lam_exp"], 1)
            own.done(TTn(A["lams"][0:1, 4:5], A["lams"][0:1, 2:3], A["lams"][0:1, 3:4], ALU.subtract))
            own.settle()
            TS(A["lams"][0:1, 5:6], A["lams"][0:1, 4:5], LAM_INIT, None, ALU.add).then_inc(S["lam_val"], 1)
            lam16, sa, sb_, sc_, sd = A["cols2"][:, 72:88], A["sp_a"][:], A["sp_b"][:], A["sp_c"][:], A["sp_d"][:]
            dve.wait_ge(S["cols_ready"], 2)
            own.done(TS(sc_, lam16, -1.0, None, ALU.mult))
            own.settle()
            TTn(sa, lam16, sc_, ALU.max).then_inc(S["sp_abs"], 1)
            dve.wait_ge(S["sp_exp"], 1)
            own.done(TS(sd, sb_, 2.0, None, ALU.add))
            own.settle()
            own.done(dve.reciprocal(sa, sd))
            own.settle()
            own.done(TTn(sb_, sb_, sa, ALU.mult))
            own.settle()
            own.done(TTn(sa, sb_, sb_, ALU.mult))
            own.settle()
            own.done(TS(sd, sa, 1.0 / 15, None, ALU.mult))
            own.settle()
            for n in (13, 11, 9, 7, 5, 3):
                own.done(STT(sd, sd, 1.0 / n, sa, ALU.add, ALU.mult))
                own.settle()
            own.done(STT(sd, sd, 1.0, sb_, ALU.add, ALU.mult))
            own.done(TS(sc_, sc_, 0.0, None, ALU.max))
            own.settle()
            own.done(STT(sd, sd, 2.0, sc_, ALU.mult, ALU.add))
            own.done(dve.tensor_copy(prm_all[:, :, 0:13].rearrange("p b m -> p m b"),
                                     A["cols2"][:, 0:104].rearrange("p (m b) -> p m b", b=NB)))
            own.settle()
            sdv = sd.rearrange("p (m b) -> p m b", b=NB)
            own.done(TS(prm_all[:, :, LAM_:LAM_ + 2].rearrange("p b m -> p m b"), sdv, 8.0, None, ALU.mult))
            own.done(TS(prm_all[:, :, NEG:NEG + 2].rearrange("p b m -> p m b"), sdv, -8.0, None, ALU.mult))
            own.done(TS(gsub_col, A["cols2"][:, 104:105], 1.0 - LAM_INIT, None, ALU.mult))
            dve.wait_ge(S["lam_spread"], 1)
            own.done(dve.tensor_copy(lam_col, ps[:, 6, 0:1]))
            split_lo(dve, Q_MOD, 0)
            dve.wait_ge(S["sqrt_x"], 1)
            own.done(dve.reciprocal(stats[:, 8:8 + TT], stats[:, 8:8 + TT]))
            own.settle()
            for t in range(TT):
                TS(x_in[:, t, :], x_in[:, t, :], stats[:, 8 + t:9 + t], None, ALU.mult).then_inc(S["xn_ready"], 1)
            for g in range(1, 4 * TT, 2):
                dve.wait_ge(S["x_turned"], g + 1)
                t, kq = g // 4, g % 4
                dve.tensor_copy(xT[:, 4 * kq:4 * kq + 4, t * P:(t + 1) * P],
                                ps[:, 4 + kq, :].rearrange("p (k n) -> p k n", k=4)).then_inc(S["xt_dve"], 1)
            with dve.Fori(0, 6) as g:
                for k in range(KT):
                    split_lo(dve, Q_MOD + g * 4, k + 1)
                dve.wait_ge(S["b_loaded"], g * 16 + 16)
                wait(dve, "m_row_free", g)
                dve.wait_ge(units_used, (Q_MOD + g * 4 + 4) * 4 + NHL)
                TTn(A["m_row"][:].rearrange("p (b n) -> p b n", b=4), ps[0:2, 0:4, :],
                    A["b_row"][:].rearrange("p (b n) -> p b n", b=4), ALU.add).then_inc(S["m_row_ready"], 1)
            dve.wait_ge(S["rows3_turned"], 1)
            own.done(dve.tensor_copy(A["cols3"][:], ps[:, 7, 0:64]))
            own.settle()
            for r in range(2):
                last = STT(A["A1"][:, r, :], A["cols3"][:, 32 * r + 16:32 * r + 32], 1.0, A["cols1"][:, 32:48],
                           ALU.add, ALU.mult)
                own.done(last) if r == 0 else last.then_inc(S["a1_ready"], 1)
            dve.wait_ge(S["a1_ready"], 1)
            for k in range(KT):
                dve.wait_ge(S["tok_hi"], k + 1)
                for r, s in ((0, slice(0, N_LAT)), (1, slice(N_LAT, N_TOK))):
                    own.done(TS(xT[:, k, s], xT[:, k, s], A["A1"][:, r, k:k + 1],
                                A["cols3"][:, 32 * r + k:32 * r + k + 1], ALU.mult, ALU.add))
                own.settle()
                TTn(lo[:, k, :], xT[:, k, :], hi[:, k, :].bitcast(F32), ALU.subtract).then_inc(S["tok_lo"], 1)
            change(dve, 1)

            with dve.Fori(0, 2) as c:
                for kq in range(4):
                    split_lo(dve, Q_V + c, kq + 1)
                wait(dve, "v_free", c)
                for t in range(TT):
                    if t < TT - 1:
                        dve.wait_ge(S["bank_done"], c * (TT - 1) + t + 1)
                    else:
                        dve.wait_ge(units_used, (Q_V + c + 1) * 4 + NHL)
                    dve.tensor_copy(v_stage[:, t, :], ps[:, t, :]).then_inc(S["bank_taken"], 1)
            with dve.Fori(0, 8) as i:
                for j in range(4):
                    split_lo(dve, Q_IN + i, j + 1)
            change(dve, 2)

            prm, att = C["prm"], C["att"]
            with dve.Fori(0, NH) as h:
                own.enter(h, PER_HEAD)
                split_lo(dve, Q_GATE + h, 1)
                dve.tensor_copy(prm[:, 0:NPRM], prm_all[:, bass.ds(h, 1), :].rearrange("p o m -> p (o m)")
                                ).then_inc(S["prm_set"], 1)
                dve.wait_ge(S["prm_set"], h + 1)
                dve.wait_ge(S["xr_loaded"], h * 16 + 16)
                xr, xc = C["xr"], C["xc"]
                spans = ((0, N_LAT), (N_LAT, N_TOK))
                for b, e in spans:
                    own.done(TS(xc[:, b:e], xr[:, b:e], prm[:, CW + 2:CW + 3], prm[:, CB:CB + 1], ALU.mult, ALU.add))
                for tap, off in ((0, -2), (1, -1), (3, 1)):
                    own.settle()
                    for b, e in spans:
                        d0, d1 = (b - off, e) if off < 0 else (b, e - off)
                        last = STT(xc[:, d0:d1], xr[:, d0 + off:d1 + off], prm[:, CW + tap:CW + tap + 1],
                                   xc[:, d0:d1], ALU.mult, ALU.add)
                        if tap == 3 and e == N_TOK:
                            last.then_inc(S["xc_ready"], 1)
                        else:
                            own.done(last)
                dve.wait_ge(S["kt_done"], h + 1)
                wait(dve, "k_new_free", h)
                dve.tensor_copy(C["k_all"][:, 0:PAST], ps[:, 4, 0:P]).then_inc(S["kt_taken"], 1)
                dve.tensor_copy(C["k_new"][:], ps[:, 7, 0:P]).then_inc(S["kt_taken"], 1)
                dve.wait_ge(S["rope_loaded"], 16)

                def rotate(name, swapped, ready, dst):
                    dve.wait_ge(S[ready], h * 80 + 80)
                    x, y = C[name], C[swapped]
                    own.done(TTn(x[:, 0:N_LAT], x[:, 0:N_LAT], C["rope"][:, 0, :], ALU.mult))
                    own.done(TTn(y[:], y[:], C["rope"][:, 1, :], ALU.mult))
                    own.settle()
                    own.done(TTn(dst, x[:, 0:N_LAT], y[:], ALU.add))

                rotate("k", "k_sw", "k_loaded", C["k_all"][:, PAST:NKEY])
                own.done(dve.tensor_copy(C["k_all"][:, NKEY:], C["k"][:, N_LAT:]))

                def lru(d):
                    dst = L[("h_f", "h_b")[d]]
                    dve.wait_ge(S["lru_at"], h * 4 + 2 * d + 2)
                    own.done(TS(L["ld"][:], L["lt"][:], 1.0, None, ALU.add))
                    own.settle()
                    own.done(dve.reciprocal(L["ld"][:], L["ld"][:]))
                    own.done(TTn(L["li"][:], L["li"][:], xc[:], ALU.mult))
                    own.settle()
                    TTn(L["lt"][:], L["lt"][:], L["ld"][:], ALU.mult).then_inc(S["lru_q"], 1)
                    if d == 0:
                        rotate("q", "q_sw", "q_loaded", C["q"][:, 0:N_LAT])
                    dve.wait_ge(S["lru_sqrt"], h * 2 + d + 1)
                    TTn(L["ld"][:], L["li"][:], L["lt"][:], ALU.mult).then_inc(S["lru_b"], 1)
                    dve.wait_ge(S["lru_b"], h * 2 + d + 1)
                    for n, (b, e) in enumerate(spans):
                        init = prm[:, H0 + d:H0 + d + 1] if n == 0 else 0.0
                        sl = slice(b, e) if d == 0 else slice(e - 1, b - 1 if b else None, -1)
                        last = dve.tensor_tensor_scan(dst[:, sl], L["la"][:, sl], L["ld"][:, sl], init, ALU.mult, ALU.add)
                        own.done(last) if n == 0 else last.then_inc(S["lru_scan"], 1)
                    dve.wait_ge(S["lru_scan"], h * 2 + d + 1)
                    end = N_TOK - 1 if d == 0 else N_LAT
                    own.done(dve.tensor_copy(state_col[:, bass.ds(h + d * NB, 1)], dst[:, end:end + 1]))

                lru(0)
                split_lo(dve, Q_GATE + h, 2)
                lru(1)
                own.done(TTn(L["h_f"][:], L["h_f"][:], L["h_b"][:], ALU.add))
                own.settle()
                dve.wait_ge(S["gelu_done"], h + 1)
                TTn(L["h_f"][:], L["h_f"][:], L["gel"][:], ALU.mult).then_inc(S["y_ready"], 1)

                def row_max(qt):
                    dve.wait_ge(S["score_done"], h * TT + qt + 1)
                    for c in range(2):
                        src = ps[:, 2 * c:2 * c + 2, 0:HALF] if qt < TT - 1 else ps[:, 2 * c, 0:P]
                        own.done(dve.tensor_reduce(att[:, 16 + c:17 + c], src, AX.XY if qt < TT - 1 else AX.X, ALU.max))
                    own.settle()
                    i = 4 * (qt % 2)
                    TS(att[:, i:i + 2], att[:, 16:18], -ATT_SCALE, None, ALU.mult).then_inc(S["score_max"], 1)

                def differ(qt):
                    dve.wait_ge(S["score_exp"], h * 2 * TT + 2 * qt + 2)
                    i = 8 + 4 * (qt % 2)
                    n = NKEY if qt < TT - 1 else P
                    p1, p2 = C["probs"][:, qt % 2, 0, 0:n], C["probs"][:, qt % 2, 1, 0:n]
                    own.done(dve.reciprocal(att[:, 20:22], att[:, i:i + 2]))
                    own.settle()
                    own.done(TTn(att[:, 22:23], att[:, 21:22], lam_col, ALU.mult))
                    own.settle()
                    own.done(TS(p2, p2, att[:, 22:23], None, ALU.mult))
                    own.settle()
                    STT(p1, p1, att[:, 20:21], p2, ALU.mult, ALU.subtract).then_inc(S["pd_ready"], 1)

                row_max(0)
                differ(0)
                split_lo(dve, Q_GATE + h, 3)
                for qt in range(1, TT):
                    row_max(qt)
                    differ(qt)
                split_lo(dve, Q_GATE + h, 4)
                dve.wait_ge(S["ms_sqrt"], h + 1)
                own.done(dve.reciprocal(C["rsd"][:], C["rsd"][:]))
                own.settle()
                wait(dve, "o_n_free", h)
                for b, s in ((0, slice(0, N_LAT)), (1, slice(N_LAT, N_TOK))):
                    STT(C["o_n"][:, s], ps[:, b, 0:s.stop - s.start], gsub_col, C["rsd"][:, s], ALU.mult, ALU.mult
                        ).then_inc(S["o_ready"], 1)
            own.leave(NH)
            change(dve, 3)

            for k in range(KT):
                dve.wait_ge(S["z_hi"], k + 1)
                TTn(lo[:, k, :], mix[:, k, :], hi[:, k, :].bitcast(F32), ALU.subtract).then_inc(S["z_lo"], 1)
            with dve.Fori(0, 4) as i:
                own.enter(i, 8)
                for j in range(4):
                    split_lo(dve, Q_AB + i, j + 1)
                    b = 4 * (j % 2)
                    dve.wait_ge(S["g_sig"], i * 4 + j + 1)
                    dve.wait_ge(S["ab_a"], i * 4 + j + 1)
                    m = mix[:, bass.ds(i * 4 + j, 1), :].rearrange("p o n -> p (o n)")
                    own.done(TTn(halves(m), ps[:, b:b + 2, 0:HALF], halves(G["gate"][:, j % 2, 0, :]), ALU.mult))
                    wait(dve, "mix_done", i * 4 + j)
                    dve.wait_ge(units_used, i * 4 + Q_AB * 4 + j + 1 + NHL)
                    own.done(TTn(halves(G["mix_b"][:]), ps[:, b + 2:b + 4, 0:HALF],
                                 halves(G["gate"][:, j % 2, 1, :]), ALU.mult))
                    own.settle()
                    TTn(m, m, G["mix_b"][:], ALU.add).then_inc(S["mix_done"], 1)
            own.leave(4)
            change(dve, 4)

            for k in range(KT):
                dve.wait_ge(S["mix_hi"], k + 1)
                TTn(lo[:, k, :], mix[:, k, :], hi[:, k, :].bitcast(F32), ALU.subtract).then_inc(S["mix_lo"], 1)
            for c in range(4):
                for kq in range(4):
                    split_lo(dve, Q_O + c, kq + 1)
                for t in range(TT):
                    o_bank_wait(dve, c, t)
                    dve.tensor_copy(t_out[:, t, c * 512:(c + 1) * 512], ps[:, t, :]).then_inc(S["o_taken"], 1)
            change(dve, 5)

            dve.tensor_reduce(stats[:, 40:40 + TT], stats[:, 16:36].rearrange("p (t c) -> p t c", c=4), AX.X, ALU.add
                              ).then_inc(S["rs1_sum"], 1)
            dve.wait_ge(S["rs1_sqrt"], 1)
            own.done(dve.reciprocal(stats[:, 40:40 + TT], stats[:, 40:40 + TT]))
            sm, aff = T["sm"], T["aff"]
            n_vec = 0
            for t in range(TT):
                if t in (0, TT - 1):
                    n_vec += 4
                    dve.wait_ge(S["vec_loaded"], n_vec * 16)
                    own.settle()
                    TTn(R1["G1"][:], R1["G1"][:], R2["row_t"][:], ALU.mult).then_inc(S["vec_ready"], 1)
                    n_vec += 1
                    dve.wait_ge(S["vec_loaded"], n_vec * 16)
                    STT(R1["A2"][:], R1["A2"][:], 1.0, R2["row_t"][:], ALU.add, ALU.mult).then_inc(S["vec_ready"], 1)
                    dve.wait_ge(S["vec_ready"], n_vec // 5 * 2)
                x = t_out[:, t, :]
                own.done(STT(x, x, stats[:, 40 + t:41 + t], R1["G1"][:], ALU.mult, ALU.mult))
                own.settle()
                dve.wait_ge(S[f"xt_loaded{t % 2}"], (t // 2 + 1) * 16)
                TTn(x, x, R1["x_t"][:, t % 2, :], ALU.add).then_inc(S["x2_ready"], 1)
                dve.wait_ge(S["x2_sqrt"], t + 1)
                own.done(dve.reciprocal(stats[:, 56 + t:57 + t], stats[:, 48 + t:49 + t]))
                own.settle()
                if t >= 2:
                    dve.wait_ge(S["h2_stored"], (t - 1) * 16)
                h2 = R2["h2"][:, t % 2, :]
                own.done(STT(h2, x, stats[:, 56 + t:57 + t], R1["A2"][:], ALU.mult, ALU.mult))
                own.settle()
                TTn(h2, h2, R1["B2"][:], ALU.add).then_inc(S["h2_ready"], 1)
                dve.wait_ge(S["logit_done"], t + 1)
                own.done(dve.tensor_reduce(sm[:, 0:1], ps[:, 4, 0:NE], AX.X, ALU.max))
                own.settle()
                TS(sm[:, 1:2], sm[:, 0:1], -1.0, None, ALU.mult).then_inc(S["logit_max"], 1)
                dve.wait_ge(S["logit_exp"], t + 1)
                own.done(dve.reciprocal(sm[:, 3:4], sm[:, 2:3]))
                own.settle()
                TS(aff[:], aff[:], sm[:, 3:4], None, ALU.mult).then_inc(S["aff_ready"], 1)
                dve.wait_ge(S["affT_done"], t + 1)
                dve.tensor_copy(T["affT"][:, t * P:(t + 1) * P], ps[0:NE, 5, 0:P]).then_inc(S["affT_taken"], 1)
            dve.wait_ge(S["affT_taken"], TT)
            for b, e, cap, at0 in ((0, N_LAT, CAP_LAT, 0), (N_LAT, N_TOK, CAP_CTX, CAP_LAT)):
                work = T["affT"][:, b:e]
                for r in range(cap // 8):
                    v8, i8 = (T[n][:, at0 + 8 * r:at0 + 8 * r + 8] for n in ("vals", "idx"))
                    own.done(dve.max(v8, work))
                    own.settle()
                    own.done(dve.max_index(i8, v8, work))
                    own.settle()
                    own.done(dve.match_replace(work, v8, work, -1.0))
                    own.settle()
            own.done(dve.tensor_copy(T["idx_f"][:], T["idx"][:]))
            own.settle()
            TS(T["idx_f"][:, CAP_LAT:], T["idx_f"][:, CAP_LAT:], float(N_LAT), None, ALU.add).then_inc(S["top_ready"], 1)
            dve.wait_ge(S["topT_done"], 1)
            own.done(dve.tensor_copy(T["val_t"][0:CAP, 0:NE], ps[0:CAP, 6, 0:NE]))
            own.done(dve.tensor_copy(T["idx_t"][0:CAP, 0:NE], ps[0:CAP, 7, 0:NE]))
            own.settle()
            change(dve, 6)

            dve.tensor_copy(T["idx_e"][0:CAP, :], T["idx_t"][0:CAP, 0:1]).then_inc(S["idx_ready"], 1)
            dve.wait_ge(S["g2_loaded"], 48)
            for r in range(2):
                TTn(Z["G2"][:, r, :], Z["G2"][:, r, :], Z["f_t"][:], ALU.mult).then_inc(S["g2_ready"], 1)

            def take_xs(e):
                dve.wait_ge(S["xs_hi_done"], e + 1)
                TTn(xs_lo[:].rearrange("p (b k) n -> p b (k n)", b=4), ps[:, 0:4, 0:4 * CAP],
                    xs_hi[:].rearrange("p (b k) n -> p b (k n)", b=4).bitcast(F32), ALU.subtract
                    ).then_inc(S["xs_lo_done"], 1)

            def expert(e, last):
                quad = Q_EXP + e * 6
                wait(dve, "ye_free", e)
                dve.tensor_copy(T["sidx"][0:CAP, :], T["idx_t"][0:CAP, bass.ds(e, 1)])
                dve.tensor_copy(T["val_e"][0:CAP, :], T["val_t"][0:CAP, bass.ds(e, 1)]).then_inc(S["val_set"], 1)
                if not last:
                    dve.wait_ge(S["xsT_done"], e + 1)
                    dve.tensor_copy(T["idx_e"][0:CAP, :], T["idx_t"][0:CAP, bass.ds(e + 1, 1)]
                                    ).then_inc(S["idx_ready"], 1)
                for k in range(KT):
                    split_lo(dve, quad, k + 1)
                dve.wait_ge(S["silu_done"], e + 1)
                h3 = E["hid"][0:CAP, :].rearrange("p (b n) -> p b n", b=2)
                TTn(h3, h3, ps[0:CAP, 2:4, :], ALU.mult).then_inc(S["hid_done"], 1)
                dve.wait_ge(S["hidT_hi"], e + 1)
                TTn(hid_lo[:].rearrange("p (b k) n -> p b (k n)", b=2), ps[:, 4:6, 0:4 * CAP],
                    hid_hi[:].rearrange("p (b k) n -> p b (k n)", b=2).bitcast(F32), ALU.subtract
                    ).then_inc(S["hidT_lo"], 1)
                for k in range(8):
                    if not (last and k == 7):
                        split_lo(dve, quad, KT + k + 1)
                    if k == 2 and not last:
                        take_xs(e + 1)
                dve.wait_ge(S["val_set"], e + 1)
                dve.wait_ge(units_used, (quad + 6) * 4 + NHL)
                TS(E["ye"][0:CAP, 1024:].rearrange("p (b n) -> p b n", b=2), ps[0:CAP, 6:8, :],
                   T["val_e"][0:CAP, :], None, ALU.mult).then_inc(S["ye_dve"], 1)

            take_xs(0)
            with dve.Fori(0, NE - 1) as e:
                expert(e, False)
            expert(NE - 1, True)
            change(dve, 7)

            for t in range(TT):
                dve.wait_ge(S["f_sqrt"], t + 1)
                own.done(dve.reciprocal(stats[:, 2:3], stats[:, 1:2]))
                own.settle()
                own.done(STT(Z["f_t"][:], Z["f_t"][:], stats[:, 2:3], Z["G2"][:, int(t == TT - 1), :],
                             ALU.mult, ALU.mult))
                own.settle()
                dve.wait_ge(S["x2_loaded"], (t + 1) * 16)
                TTn(Z["f_t"][:], Z["f_t"][:], Z["x2_t"][:], ALU.add).then_inc(S["y_done"], 1)
            dve.wait_ge(S["state_turned"], 1)
            dve.tensor_copy(state_rows[:], ps[0:16, 0, 0:P]).then_inc(S["state_row"], 1)

        @block.tensor
        def _(pe):
            pe.sem_inc(units_used, NHL)

            def turn(out, in_, n=P):
                return pe.transpose(out, in_, ident[0:n, 0:n])

            pe.wait_ge(par_loaded, N_PAR * 16)
            turn(ps[:, 7, 0:48], A["rows1"][:], 48).then_inc(S["rows_turned"], 1)
            turn(ps[:, 7, 128:233], A["rows2"][:], 105).then_inc(S["rows_turned"], 1)
            pe.wait_ge(S["lam_val"], 1)
            pe.wait_ge(S["const_set"], 1)
            pe.matmul(ps[:, 6, 0:1], A["ones_row"][:], A["lams"][0:1, 5:6], start=True, stop=True
                      ).then_inc(S["lam_spread"], 1)
            for t in range(TT):
                pe.wait_ge(S["xn_ready"], t + 1)
                for kq in range(4):
                    if t:
                        pe.wait_ge(S[("xt_act", "xt_dve")[kq % 2]], 2 * (t - 1) + kq // 2 + 1)
                    for k in range(4 * kq, 4 * kq + 4):
                        last = turn(ps[:, 4 + kq, (k % 4) * P:(k % 4 + 1) * P], x_in[:, t, k * P:(k + 1) * P])
                    last.then_inc(S["x_turned"], 1)
            pe.wait_ge(S["c_ready"], 1)
            with pe.Fori(0, 6) as g:
                wait(pe, "m_row_ready", g)
                for k in range(KT):
                    unit_wait(pe, Q_MOD + g * 4, k)
                    for n in range(4):
                        s = slice(n * 512, (n + 1) * 512)
                        last = three(pe, ps[0:2, n, :], c_hi[:, k, :], c_lo[:, k, :],
                                     w_hi[:, k % 2, s], w_lo[:, k % 2, s], k == 0, k == KT - 1)
                    last.then_inc(units_used, 1)
            pe.wait_ge(S["rows3_loaded"], 64)
            turn(ps[:, 7, 0:64], A["rows3"][:], 64).then_inc(S["rows3_turned"], 1)
            change(pe, 1)

            def wide(quad, c, first_bank_free, out_sem, tok_wait):
                for kq in range(4):
                    unit_wait(pe, quad, kq)
                    for kk in range(4):
                        k = 4 * kq + kk
                        tok_wait(k)
                        s = slice(kk * 512, (kk + 1) * 512)
                        for t in range(TT):
                            if k == 0:
                                first_bank_free(t)
                            ts = slice(t * P, (t + 1) * P)
                            last = three(pe, ps[:, t, :], hi[:, k, ts], lo[:, k, ts], w_hi[:, kq % 2, s],
                                         w_lo[:, kq % 2, s], k == 0, k == KT - 1)
                            if k == KT - 1 and t < TT - 1:
                                last.then_inc(out_sem, 1)
                    last.then_inc(units_used, 1)

            pe.wait_ge(S["tok_lo"], KT)
            with pe.Fori(0, 2) as c:
                wide(Q_V + c, c, lambda t: wait(pe, "bank_taken", c * TT + t + 1 - TT), S["bank_done"], lambda k: None)

            def unit_piece(j, half, ks, bank):
                ms = slice(half * HALF, (half + 1) * HALF)
                for k in ks:
                    s = slice(k * P, (k + 1) * P)
                    wh, wl = w_hi[:, j % 2, s], w_lo[:, j % 2, s]
                    out = ps[:, bank, 0:HALF]
                    pe.matmul(out, wl, hi[:, k, ms], start=(k % 16 == 0), stop=False)
                    pe.matmul(out, wh, lo[:, k, ms], start=False, stop=False)
                    last = pe.matmul(out, wh, hi[:, k, ms], start=False, stop=(k == KT - 1))
                return last

            with pe.Fori(0, 8) as i:
                for j in range(4):
                    unit_wait(pe, Q_IN + i, j)
                    for half in range(2):
                        wait(pe, "in_taken", (i * 4 + j) * 2 + half - 1)
                        last = unit_piece(j, half, range(KT), 5 + half)
                        last.then_inc(S["in_a_done"] if half == 0 else units_used, 1)
            change(pe, 2)

            with pe.Fori(0, NH) as h:
                def keys():
                    pe.wait_ge(S["kv_loaded"], h * 48 + 48)
                    pe.wait_ge(S["k_loaded"], h * 80 + 80)
                    wait(pe, "pdT_taken", h * TT)
                    turn(ps[:, 4, 0:P], C["k_past"][:])
                    turn(ps[:, 7, 0:P], C["k"][:, N_LAT:]).then_inc(S["kt_done"], 1)

                def lru(d):
                    if d == 0:
                        pe.wait_ge(S["xc_ready"], h + 1)
                        pe.wait_ge(S["lruw_loaded"], h * 64 + 64)
                        wait(pe, "o_ready", h * 2)
                    else:
                        pe.wait_ge(S["lru_sig"], h * 4 + 2)
                    for i in range(2):
                        for half in range(2):
                            last = pe.matmul(ps[:, 2 * i + half, 0:HALF], C["lru_w"][:, 2 * d + i, :],
                                             C["xc"][:, half * HALF:(half + 1) * HALF], start=True, stop=True)
                    last.then_inc(S["lru_mm"], 1)

                def scores(qt):
                    if qt == 0:
                        pe.wait_ge(S["lru_sig"], h * 4 + 4)
                        pe.wait_ge(S["lru_q"], h * 2 + 2)
                    else:
                        pe.wait_ge(S["score_exp"], h * 2 * TT + 2 * qt)
                    for c in range(2):
                        rows = slice(c * HD, (c + 1) * HD)
                        q = C["q"][rows, qt * P:(qt + 1) * P]
                        if qt < TT - 1:
                            for half in range(2):
                                last = pe.matmul(ps[:, 2 * c + half, 0:HALF], q,
                                                 C["k_all"][rows, half * HALF:(half + 1) * HALF], start=True, stop=True)
                        else:
                            last = pe.matmul(ps[:, 2 * c, 0:P], q, C["k_all"][rows, NKEY:], start=True, stop=True)
                    last.then_inc(S["score_done"], 1)

                def turn_probs(qt):
                    pe.wait_ge(S["pd_ready"], h * TT + qt + 1)
                    if qt == 0:
                        pe.wait_ge(S["kt_taken"], h * 2 + 2)
                    else:
                        wait(pe, "pdT_taken", h * TT + qt)
                    p = C["probs"][:, qt % 2, 0, :]
                    for kt in range(5 if qt < TT - 1 else 1):
                        out = ps[:, 4, kt * P:(kt + 1) * P] if kt < 4 else ps[:, 7, 0:P]
                        last = turn(out, p[:, kt * P:(kt + 1) * P])
                    last.then_inc(S["pdT_done"], 1)

                def values():
                    wait(pe, "pdT_taken", h * TT + TT)
                    for kt in range(TT):
                        pe.matmul(ps[:, 0, :], C["v"][:, kt, :], C["pT"][:, kt, :], start=(kt == 0), stop=(kt == TT - 1))
                    pe.matmul(ps[:, 1, 0:P], C["v"][:, TT, :], C["pT_ctx"][:], start=True, stop=True
                              ).then_inc(S["av_done"], 1)

                def mean_square():
                    pe.wait_ge(S["o_sq"], h + 1)
                    pe.matmul(ps[:, 2, :], mean_mat[:], C["probs"][:, 0, 0, 0:N_LAT], start=True, stop=True)
                    pe.matmul(ps[:, 3, 0:P], mean_mat[:], C["probs"][:, 0, 0, N_LAT:], start=True, stop=True
                              ).then_inc(S["ms_done"], 1)

                after = {1: [keys], 2: [lambda: lru(0)], 4: [lambda: lru(1)], 6: [lambda: scores(0)],
                         7: [lambda: scores(1)], 8: [lambda: turn_probs(0), lambda: scores(2)],
                         9: [lambda: turn_probs(1), lambda: scores(3)], 10: [lambda: turn_probs(2), lambda: scores(4)],
                         11: [lambda: turn_probs(3)], 12: [lambda: turn_probs(4)], 13: [values], 14: [mean_square]}
                for piece in range(16):
                    j, half, part = piece // 4, piece % 4 // 2, piece % 2
                    if part == 0:
                        if half == 0:
                            unit_wait(pe, Q_GATE + h, j)
                        wait(pe, "gate_taken", (h * 4 + j) * 2 + half - 1)
                    last = unit_piece(j, half, range(8 * part, 8 * part + 8), 5 + half)
                    if part == 1:
                        last.then_inc(S["gate_a_done"] if half == 0 else units_used, 1)
                    for step in after.get(piece, []):
                        step()
            change(pe, 3)

            pe.wait_ge(S["z_lo"], KT)
            with pe.Fori(0, 4) as i:
                for j in range(4):
                    unit_wait(pe, Q_AB + i, j)
                    wait(pe, "mix_done", i * 4 + j - 1)
                    for br in range(2):
                        for half in range(2):
                            ms = slice(half * HALF, (half + 1) * HALF)
                            out = ps[:, 4 * (j % 2) + 2 * br + half, 0:HALF]
                            for k in range(8 * br, 8 * br + 8):
                                s = slice(k * P, (k + 1) * P)
                                wh, wl = w_hi[:, j % 2, s], w_lo[:, j % 2, s]
                                pe.matmul(out, wl, hi[:, k, ms], start=(k % 8 == 0), stop=False)
                                pe.matmul(out, wh, lo[:, k, ms], start=False, stop=False)
                                last = pe.matmul(out, wh, hi[:, k, ms], start=False, stop=(k % 8 == 7))
                        last.then_inc(S["ab_a"] if br == 0 else units_used, 1)
            change(pe, 4)

            for c in range(4):
                wide(Q_O + c, c, lambda t: wait(pe, "o_taken", (c - 1) * TT + t + 1), S["bank_done"],
                     lambda k: pe.wait_ge(S["mix_lo"], k + 1) if c == 0 else None)
            change(pe, 5)

            pe.wait_ge(S["wr_loaded"], 16)
            for t in range(TT):
                pe.wait_ge(S["h2_ready"], t + 1)
                for k in range(KT):
                    last = turn(ps[:, k // 4, (k % 4) * P:(k % 4 + 1) * P], R2["h2"][:, t % 2, k * P:(k + 1) * P])
                last.then_inc(S["h2T_done"], 1)
                pe.wait_ge(S["h2T_taken"], t + 1)
                for k in range(KT):
                    last = pe.matmul(ps[:, 4, 0:NE], R2["h2T"][:, k, :], T["wr"][:, k, :], start=(k == 0),
                                     stop=(k == KT - 1))
                last.then_inc(S["logit_done"], 1)
                pe.wait_ge(S["aff_ready"], t + 1)
                if t:
                    pe.wait_ge(S["affT_taken"], t)
                turn(ps[0:NE, 5, 0:P], T["aff"][:]).then_inc(S["affT_done"], 1)
            pe.wait_ge(S["top_ready"], 1)
            turn(ps[0:CAP, 6, 0:NE], T["vals"][:], NE)
            turn(ps[0:CAP, 7, 0:NE], T["idx_f"][:], NE).then_inc(S["topT_done"], 1)
            change(pe, 6)

            def turn_xs(e):
                pe.wait_ge(S["gathered"], e * 16 + 16)
                for k in range(KT):
                    last = turn(ps[:, k // 4, (k % 4) * CAP:(k % 4 + 1) * CAP], E["xs"][0:CAP, k * P:(k + 1) * P], CAP)
                last.then_inc(S["xsT_done"], 1)

            def expert(e, last_one):
                quad = Q_EXP + e * 6
                pe.wait_ge(S["xs_lo_done"], e + 1)
                for k in range(KT):
                    unit_wait(pe, quad + k // 4, k % 4)
                    for n in range(4):
                        s = slice(n * 512, (n + 1) * 512)
                        last = three(pe, ps[0:CAP, n, :], xs_hi[:, k, :], xs_lo[:, k, :],
                                     w_hi[:, k % 2, s], w_lo[:, k % 2, s], k == 0, k == KT - 1)
                    last.then_inc(units_used, 1)
                pe.wait_ge(S["hid_done"], e + 1)
                wait(pe, "ye_act", e)
                wait(pe, "ye_dve", e)
                for k in range(8):
                    last = turn(ps[:, 4 + k // 4, (k % 4) * CAP:(k % 4 + 1) * CAP],
                                E["hid"][0:CAP, k * P:(k + 1) * P], CAP)
                last.then_inc(S["hidT_done"], 1)
                pe.wait_ge(S["hidT_lo"], e + 1)
                for k in range(8):
                    unit_wait(pe, quad + 4 + k // 4, k % 4)
                    for n in range(4):
                        s = slice(n * 512, (n + 1) * 512)
                        last = three(pe, ps[0:CAP, 4 + n, :], hid_hi[:, k, :], hid_lo[:, k, :],
                                     w_hi[:, k % 2, s], w_lo[:, k % 2, s], k == 0, k == 7)
                    last.then_inc(units_used, 1)
                    if k == 1 and not last_one:
                        turn_xs(e + 1)

            turn_xs(0)
            with pe.Fori(0, NE - 1) as e:
                expert(e, False)
            expert(NE - 1, True)
            change(pe, 7)
            turn(ps[0:16, 0, 0:P], state_col[:]).then_inc(S["state_turned"], 1)


_INS = ["x_prompt", "x_sample", "cache_k", "cache_v", "state_rnn", "c", "c_ctx", "w_mod", "b_mod", "g_pre1", "g_post1",
        "g_pre2", "g_post2", "w_in", "conv_w", "conv_b", "lru_wr", "lru_br", "lru_wi", "lru_bi", "lru_lam", "lam_q1",
        "lam_k1", "lam_q2", "lam_k2", "g_sub", "w_a_out", "w_b_out", "w_o", "w_router", "w_e_gate", "w_e_up",
        "w_e_down"]
_OUTS = [(1, N_CTX, D), (1, N_LAT, D), (1, 1, N_CTX, NH, 2 * HD), (1, 1, N_CTX, NH, 2 * HD), (1, 1, 2, D_RNN)]


def kernel(**inputs):
    import concourse.bacc as bacc
    from concourse.bass_utils import run_bass_kernel_spmd

    nc = bacc.Bacc("TRN2", target_bir_lowering=False, num_devices=1)
    given = {n: np.ascontiguousarray(inputs[n]) for n in _INS}
    given["rope"] = rope_tables()
    given["ident"] = np.eye(P, dtype=np.float32)
    arrays, aps = {}, {}
    for n, x in given.items():
        arrays[f"in_{n}"] = x
        aps[n] = nc.dram_tensor(f"in_{n}", x.shape, mybir.dt.from_np(x.dtype), kind="ExternalInput").ap()
    outs = [nc.dram_tensor(f"out_{i}", s, F32, kind="ExternalOutput").ap() for i, s in enumerate(_OUTS)]
    trunk(nc, aps, *outs)
    r = run_bass_kernel_spmd(nc, [arrays], core_ids=[0])
    return tuple(r.results[0][f"out_{i}"] for i in range(len(_OUTS)))
```

```python
from contextlib import ExitStack

import numpy as np

import concourse.bass as bass
from concourse import mybir

F32 = mybir.dt.float32
F32R = mybir.dt.float32r
U32 = mybir.dt.uint32
ALU = mybir.AluOpType
ACT = mybir.ActivationFunctionType
AX = mybir.AxisListType

P = 128
D = 2048
N_LAT, N_CTX = 512, 128
N_TOK = N_LAT + N_CTX
TT = N_TOK // P
HALF = N_TOK // 2
KT = D // P
D_RNN = 1024
NB = D_RNN // P
NH, HD = 8, 64
PAST = 128
NKEY = PAST + N_LAT
NE = 16
D_EXP = 1024
CAP_LAT, CAP_CTX = 2 * N_LAT // NE, 2 * N_CTX // NE
CAP = CAP_LAT + CAP_CTX
EPS = 1e-6
ATT_SCALE = HD ** -0.5
LAM_INIT = 0.2
GRID_W = 64
V_COL, GATE_COL = 4096, 5120

NRAW = 4
NHL = 2
INC = 32
QUADS = [24, 2, 8, 8, 4, 4, NE * 6]
Q_MOD, Q_V, Q_IN, Q_GATE, Q_AB, Q_O, Q_EXP = (sum(QUADS[:i]) for i in range(7))

CW, CB, BR, BI, LAM_, H0, NEG = 0, 4, 5, 7, 9, 11, 13
NPRM = 15
N_PAR = 11
PER_HEAD = 44


def rope_tables():
    pos = np.arange(N_LAT)
    row, col = (pos // GRID_W).astype(np.float32), (pos % GRID_W).astype(np.float32)
    axis = HD // 2
    inv = (np.float32(10000.0) ** (-np.arange(0, axis, 2, dtype=np.float32) / np.float32(axis))).astype(np.float32)
    ang = np.concatenate([row[:, None] * inv, col[:, None] * inv], axis=-1).astype(np.float32)
    f = np.arange(P) % (HD // 2)
    sign = np.where(np.arange(P) % HD < HD // 2, -1.0, 1.0).astype(np.float32)
    return np.stack([np.cos(ang).T[f], np.sin(ang).T[f] * sign[:, None]], axis=1).astype(np.float32)


class Own:

    def __init__(self, eng, sem):
        self.eng, self.sem, self.n, self.off = eng, sem, 0, 0

    def done(self, ins):
        ins.then_inc(self.sem, 1)
        self.n += 1

    def settle(self):
        self.eng.wait_ge(self.sem, self.n + self.off)

    def enter(self, it, per):
        self.start, self.per, self.off = self.n, per, it * per

    def leave(self, count):
        assert self.n - self.start == self.per, (self.n - self.start, self.per)
        self.n, self.off = self.start + count * self.per, 0


def trunk(nc, a, out_ctx, out_lat, out_k, out_v, out_state):
    ctx = ExitStack()
    with ctx:
        base = -(-nc.sbuf_base // 64) * 64
        top = {"at": base}

        def at(name, shape, dt, offset):
            size = int(np.prod(shape[1:])) * 4
            assert offset % 32 == 0 and offset + size <= nc.sbuf_usable_end, (name, offset, size)
            return nc.alloc_sbuf_tensor_at(name, shape, dt, offset=offset)

        def area(size):
            o = top["at"]
            top["at"] += -(-size // 64) * 64
            return o

        def sem(name):
            return ctx.enter_context(nc.semaphore(name))

        def dram(name, shape):
            return nc.dram_tensor(name, shape, F32).ap()

        UB = D * 4
        raw = at("raw", [P, NRAW, D], F32, area(NRAW * UB))
        w_hi = at("w_hi", [P, NHL, D], F32R, area(NHL * UB))
        w_lo = at("w_lo", [P, NHL, D], F32R, area(NHL * UB))
        ra, rb = area(KT * N_TOK * 4), area(KT * N_TOK * 4)
        hi = at("hi", [P, KT, N_TOK], F32R, ra)
        lo = at("lo", [P, KT, N_TOK], F32R, rb)
        ident = at("ident", [P, P], F32, area(P * 4))
        mean_mat = at("mean_mat", [P, P], F32, area(P * 4))
        prm_all = at("prm_all", [P, NB, NPRM], F32, area(NB * NPRM * 4))
        misc = at("misc", [P, 32], F32, area(128))
        stats = at("stats", [P, 64], F32, area(256))
        state_col = at("state_col", [P, 2 * NB], F32, area(64))
        eps_col, lam_col, gsub_col, ones_col = (misc[:, i:i + 1] for i in range(4))
        s0 = top["at"]
        s_end = nc.sbuf_usable_end

        PLACED = {}

        def place(at0, items):
            o, made = at0, {}
            for name, shape, dt in items:
                made[name] = at(name, shape, dt, o)
                PLACED[name] = o
                o += -(-int(np.prod(shape[1:])) * 4 // 64) * 64
            assert o <= s_end, (o, s_end)
            return made

        zT = at("zT", [P, KT, N_TOK], F32, rb)
        x_in = at("x_in", [P, TT, D], F32, ra)
        xT = at("xT", [P, KT, N_TOK], F32, rb)
        A = place(s0, [("b_row", [2, D], F32), ("m_row", [2, D], F32), ("junk0", [P, D], F32),
                       ("zero", [P, D], F32), ("rows1", [48, P], F32), ("rows2", [105, P], F32),
                       ("rows3", [64, P], F32), ("cols1", [P, 48], F32), ("cols2", [P, 105], F32),
                       ("cols3", [P, 64], F32), ("sc", [P, 32], F32), ("lamv", [1, 4, 64], F32),
                       ("lamp", [1, 2, 64], F32), ("lams", [1, 8], F32), ("ones_row", [1, P], F32),
                       ("sp_a", [P, 16], F32), ("sp_b", [P, 16], F32), ("sp_c", [P, 16], F32),
                       ("sp_d", [P, 16], F32), ("A1", [P, 2, KT], F32)])
        A["diag"] = at("diag", [P, 2, P], F32, s0 + 50048 + 256)
        c_hi = at("c_hi", [P, KT, 2], F32R, s0 + 50048)
        c_lo = at("c_lo", [P, KT, 2], F32R, s0 + 50048 + 128)
        assert PLACED["A1"] + 128 <= s0 + 50048
        v_stage = at("v_stage", [P, TT, 512], F32, s0)
        stage = at("stage", [P, 2, N_TOK], F32, s0 + TT * 512 * 4)
        C = place(s0, [("rope", [P, 2, N_LAT], F32), ("perm", [P, P], F32), ("q_in", [P, N_TOK], F32),
                       ("q", [P, N_TOK], F32), ("k", [P, N_TOK], F32), ("turned", [P, N_LAT], F32),
                       ("k_all", [P, PAST + N_TOK], F32),
                       ("k_past", [P, P], F32), ("k_new", [P, P], F32), ("v", [P, TT + 1, P], F32),
                       ("xr", [P, N_TOK], F32), ("xc", [P, N_TOK], F32), ("gr", [P, N_TOK], F32),
                       ("rsd", [P, N_TOK], F32), ("o_n", [P, N_TOK], F32), ("lru_w", [P, 4, P], F32),
                       ("prm", [P, 16], F32), ("att", [P, 32], F32), ("g_stage", [P, 2, N_TOK], F32),
                       ("probs", [P, 2, 2, N_TOK], F32), ("pT", [P, TT, N_LAT], F32), ("pT_ctx", [P, P], F32)])
        reg1 = PLACED["probs"]
        L = place(reg1, [(n, [P, N_TOK], F32) for n in
                         ("lr", "li", "la", "lt", "ld", "h_f", "h_b", "gel")])
        mix = at("mix", [P, KT, N_TOK], F32, s0)
        G = place(s0 + KT * N_TOK * 4, [("gate", [P, 2, 2, N_TOK], F32), ("mix_b", [P, N_TOK], F32)])
        t_out = at("t_out", [P, TT, D], F32, s0)
        late = s0 + TT * UB + 5120
        junk_o = at("junk_o", [P, 512], F32, s0 + TT * UB)
        VL = at("vec_lat", [P, 2, D], F32, late)
        R1 = place(ra, [("shift_lat", [P, D], F32), ("vec_ctx", [P, 2, D], F32), ("x_t", [P, 2, D], F32)])
        R2 = place(rb, [("h2", [P, 2, D], F32), ("h2T", [P, KT, P], F32), ("junk1", [P, D], F32),
                        ("shift_ctx", [P, D], F32)])
        T = place(s0 + TT * D * 4, [("aff", [P, 16], F32), ("affT", [NE, N_TOK], F32), ("vals", [NE, CAP], F32),
                                    ("idx", [NE, CAP], U32), ("idx_f", [NE, CAP], F32), ("wr", [P, KT, NE], F32),
                                    ("sm", [P, 8], F32), ("sidx", [P, 1], U32),
                                    ("val_t", [P, NE + 1], F32), ("idx_t", [P, NE + 1], U32),
                                    ("val_e", [P, 1], F32), ("idx_e", [P, 1], U32)])
        E = place(ra, [("xs", [P, D], F32), ("ye", [P, D], F32), ("hid", [P, D_EXP], F32), ("junk_e", [P, D_EXP], F32)])
        xs_hi = at("xs_hi", [P, KT, CAP], F32R, ra + 24576)
        xs_lo = at("xs_lo", [P, KT, CAP], F32R, ra + 24576 + 5120)
        hid_hi = at("hid_hi", [P, 8, CAP], F32R, ra + 24576 + 10240)
        hid_lo = at("hid_lo", [P, 8, CAP], F32R, ra + 24576 + 12800)
        raw2 = at("raw2", [P, NRAW, D], F32, rb)
        Z = place(ra, [("f", [P, TT, D], F32)])
        junk2 = at("junk2", [P, D], F32, rb)
        G2 = at("G2", [P, 2, D], F32, late)
        assert PLACED["idx_e"] + 64 <= late, PLACED["idx_e"] - s0 - TT * UB
        state_rows = at("state_rows", [2 * NB, P], F32, rb + UB)
        vec_rows = at("vec_rows", [96, P], F32, s0 + 51200)
        gain_rows = at("gain_rows", [96, P], F32, s0 + 51712)
        ps = ctx.enter_context(nc.psum_tensor("ps", [P, 8, 512], F32))

        d_mod = dram("d_mod", [2, 6 * D])
        d_proj = dram("d_proj", [72 * P, N_TOK])
        d_v = dram("d_v", [N_TOK, D_RNN])
        d_z = dram("d_z", [KT * P, N_TOK])
        d_vec = dram("d_vec", [6, D])
        d_h2 = dram("d_h2", [N_TOK, D])
        d_f = dram("d_f", [N_TOK, D])

        raw_loaded = [sem(f"raw_loaded{i}") for i in range(2 * NRAW)]
        hi_ready = sem("hi_ready")
        lo_ready = sem("lo_ready")
        halves_used = sem("halves_used")
        phase = sem("phase")
        pool_own, dve_own, act_own = sem("pool_own"), sem("dve_own"), sem("act_own")
        par_loaded, x_lat_loaded, x_ctx_loaded = sem("par_loaded"), sem("x_lat_loaded"), sem("x_ctx_loaded")
        S = {n: sem(n) for n in (
            "const_set", "c_loaded", "rows_turned", "cols_ready", "c_act", "c_ready", "small_dve", "small_act",
            "lam_val", "lam_spread",
            "sqrt_x", "xn_ready", "x_turned", "xt_act", "xt_dve", "b_loaded", "m_row_ready", "m_stored",
            "zero_stored", "rows3_loaded", "rows3_turned", "a1_ready", "tok_hi", "tok_lo",
            "bank_done", "bank_taken", "v_stored", "in_a_done", "in_taken", "in_stored",
            "rope_loaded", "xr_loaded", "lruw_loaded", "gr_loaded", "q_loaded", "k_loaded", "kp_loaded",
            "v_loaded", "prm_set",
            "xc_ready", "rot_done", "rot_read", "qk_ready", "kt_done", "kt_taken", "knew_stored", "gate_a_done",
            "gate_taken",
            "gate_stored", "lru_mm", "lru_sig", "lru_at", "lru_q", "lru_sqrt", "lru_b", "lru_scan",
            "gelu_done", "y_ready", "y_stored", "score_done", "score_max", "score_exp", "pd_ready", "pdT_done",
            "pdT_taken", "av_done", "o_sq", "ms_done", "ms_sqrt", "o_ready", "o_stored",
            "z_loaded0", "z_loaded1", "g_loaded0", "g_loaded1", "g_sig", "ab_a", "mix_done", "split_in_hi",
            "split_in_lo",
            "o_taken", "rs1_sum", "rs1_sqrt",
            "vrow_loaded", "vec_ready", "vec_stored", "vec_lat_loaded", "shift_loaded", "vec_ctx_loaded",
            "xt_loaded0", "xt_loaded1", "x2_ready", "x2_sqrt", "h2_ready",
            "h2_stored0", "h2_stored1", "h2T_done", "h2T_taken", "logit_done", "logit_max", "logit_exp",
            "aff_ready", "affT_done",
            "affT_taken", "top_ready", "topT_done", "wr_loaded",
            "idx_ready", "gathered", "xsT_done", "xs_hi_done", "xs_lo_done", "silu_done", "hid_done", "hidT_done",
            "hidT_hi", "hidT_lo", "val_set", "ye_ready", "scattered", "g2_loaded",
            "f_loaded0", "f_loaded1", "f_loaded2", "f_sqrt", "y_done", "y_out", "passed", "m_row_free", "v_free",
            "stage_free", "g_stage_free", "k_new_free", "o_n_free", "ye_free", "state_turned", "state_row",
            "state_stored")}

        CREDIT = {"m_row_ready": 1, "m_row_free": 1, "bank_taken": TT, "v_free": 1, "in_taken": 2, "stage_free": 2,
                  "gate_taken": 2, "g_stage_free": 2, "k_new_free": 1, "o_ready": 1, "o_n_free": 1, "pdT_taken": 1,
                  "mix_done": 2, "o_taken": TT, "ye_ready": 2, "ye_free": 1}

        def give(eng, *names):
            for n in names:
                eng.sem_inc(S[n], CREDIT[n])

        def wait(eng, name, value):
            eng.wait_ge(S[name], value + CREDIT.get(name, 0))

        def used(n):
            return 2 * n + 2 * NHL

        def half_of(p):
            return slice(p * 1024, (p + 1) * 1024)

        def split_hi(act, quad, j, fine=False):
            quad, j = quad + j // NRAW, j % NRAW
            u = quad * NRAW + j
            act.wait_ge(raw_loaded[j], (quad + 1) * INC)
            for p in range(2 if fine else 1):
                act.wait_ge(halves_used, 2 * u + (p + 1 if fine else 2))
                s = half_of(p) if fine else slice(0, D)
                act.activation(w_hi[:, j % NHL, s], raw[:, j, s], ACT.Copy).then_inc(hi_ready, 1 if fine else 2)

        def split_lo(dve, quad, j, fine=False):
            quad, j = quad + j // NRAW, j % NRAW
            u = quad * NRAW + j
            for p in range(2 if fine else 1):
                dve.wait_ge(hi_ready, 2 * u + (p + 1 if fine else 2))
                s = half_of(p) if fine else slice(0, D)
                dve.tensor_tensor(w_lo[:, j % NHL, s], raw[:, j, s], w_hi[:, j % NHL, s].bitcast(F32),
                                  ALU.subtract).then_inc(lo_ready, 1 if fine else 2)

        def raw_slot(k):
            return raw[:, k % 8, :] if k % 8 < NRAW else raw2[:, k % 8 - NRAW, :]

        def exp_loads(e, k):
            return ((Q_EXP if k % 8 < NRAW else 0) + 3 * e + k // 8 + 1) * INC

        def exp_split_hi(act, e, k):
            u = Q_EXP * NRAW + e * 24 + k
            act.wait_ge(raw_loaded[k % 8], exp_loads(e, k))
            for p in range(2):
                act.wait_ge(halves_used, 2 * u + p + 1)
                act.activation(w_hi[:, k % NHL, half_of(p)], raw_slot(k)[:, half_of(p)], ACT.Copy
                               ).then_inc(hi_ready, 1)

        def exp_split_lo(dve, e, k):
            u = Q_EXP * NRAW + e * 24 + k
            for p in range(2):
                dve.wait_ge(hi_ready, 2 * u + p + 1)
                dve.tensor_tensor(w_lo[:, k % NHL, half_of(p)], raw_slot(k)[:, half_of(p)],
                                  w_hi[:, k % NHL, half_of(p)].bitcast(F32), ALU.subtract).then_inc(lo_ready, 1)

        def unit_wait(pe, quad, j):
            pe.wait_ge(lo_ready, 2 * NRAW + 2 * (quad * NRAW + j + 1))

        def by_halves(pe, u, slot, out, s_hi, s_lo, start, stop):
            for p in range(2):
                pe.wait_ge(lo_ready, 2 * NRAW + 2 * u + p + 1)
                for n in (2 * p, 2 * p + 1):
                    s = slice(n * 512, (n + 1) * 512)
                    last = three(pe, out[:, n, :], s_hi, s_lo, w_hi[:, slot, s], w_lo[:, slot, s], start, stop)
                last.then_inc(halves_used, 1)

        def change(eng, k):
            eng.drain().then_inc(phase, 1)
            eng.wait_ge(phase, 4 * k)

        def o_bank_wait(eng, c, t):
            if t < TT - 1:
                eng.wait_ge(S["bank_done"], 2 * (TT - 1) + c * (TT - 1) + t + 1)
            else:
                eng.wait_ge(halves_used, used((Q_O + c + 1) * 4))

        def halves(tile):
            return tile.rearrange("p (a n) -> p a n", a=2)

        def three(pe, out, s_hi, s_lo, m_hi, m_lo, start, stop):
            pe.matmul(out, s_lo, m_hi, start=start, stop=False)
            pe.matmul(out, s_hi, m_lo, start=False, stop=False)
            return pe.matmul(out, s_hi, m_hi, start=False, stop=stop)

        def leave(pe):
            pe.drain().then_inc(phase, 1)

        block = ctx.enter_context(nc.Block())

        @block.sync
        def _(sp):
            def load(quad, j, parts):
                sp.wait_ge(lo_ready, 2 * (quad * NRAW + j + 1))
                for dst, src in parts:
                    sp.dma_start(dst, src).then_inc(raw_loaded[j], INC // 2)

            def rows(w, k, c0):
                return [(slice(0, 1024), w[bass.ds(k * P, P), bass.ds(c0, 1024)]),
                        (slice(1024, 2048), w[bass.ds(k * P, P), bass.ds(c0 + 1024, 1024)])]

            w_mod, w_in = a["w_mod"][0], a["w_in"][0]
            with sp.Fori(0, 6) as g:
                for k in range(KT):
                    load(Q_MOD + g * 4 + k // NRAW, k % NRAW,
                         [(raw[:, k % NRAW, s], src) for s, src in rows(w_mod, k, g * D)])

            def wide(w, j, kq, c0):
                v = raw[:, j, :].rearrange("p (k n) -> p k n", k=4)
                return [(v[:, 2 * i:2 * i + 2, :],
                         w[(4 * kq + 2 * i) * P:(4 * kq + 2 * i + 2) * P, bass.ds(c0, 512)].rearrange(
                             "(k p) n -> p k n", p=P)) for i in range(2)]

            def tall(pieces, j, c0):
                v = raw[:, j, :].rearrange("p (k n) -> p k n", k=KT)
                return [(v[:, 8 * i:8 * i + 8, :], w[:, bass.ds(c0, P)].rearrange("(k p) n -> p k n", p=P))
                        for i, w in enumerate(pieces)]

            with sp.Fori(0, 2) as c:
                for kq in range(4):
                    load(Q_V + c, kq, wide(w_in, kq, kq, V_COL + c * 512))
            w_in2 = [w_in[0:D // 2], w_in[D // 2:D]]
            with sp.Fori(0, 8) as i:
                for j in range(4):
                    load(Q_IN + i, j, tall(w_in2, j, (i * 4 + j) * P))
            with sp.Fori(0, 8) as i:
                for j in range(4):
                    load(Q_GATE + i, j, tall(w_in2, j, GATE_COL + (i * 4 + j) * P))

            def w_ab(i):
                for j in range(4):
                    load(Q_AB + i, j, tall([a["w_a_out"][0], a["w_b_out"][0]], j, (i * 4 + j) * P))

            w_ab(0)
            zs = d_z.rearrange("(k p) n -> p k n", p=P)
            sp.wait_ge(halves_used, used(Q_AB * 4))
            sp.wait_ge(S["y_stored"], NB * 16)
            for i in range(2):
                ks = slice(4 * i, 4 * i + 4)
                sp.dma_start(zT[:, ks, :], zs[:, ks, :]).then_inc(S[f"z_loaded{i}"], 16)
            sp.wait_ge(S["z_loaded0"], 16)
            sp.wait_ge(S["o_stored"], (NH - 1) * 16)
            sp.dma_start(zT[:, NB:KT - 1, :], zs[:, NB:KT - 1, :]).then_inc(S["z_loaded0"], 16)
            sp.wait_ge(S["z_loaded1"], 16)
            sp.wait_ge(S["o_stored"], NH * 16)
            sp.dma_start(zT[:, KT - 1, :], zs[:, KT - 1, :]).then_inc(S["z_loaded1"], 16)
            with sp.Fori(1, 4) as i:
                w_ab(i)
            def row(x):
                return x.to_broadcast([P, D])

            def w_o(c):
                for kq in range(4):
                    load(Q_O + c, kq, wide(a["w_o"][0], kq, kq, c * 512))

            w_o(0)
            sp.wait_ge(phase, 4 * 4)
            for i, v in enumerate((2, 0)):
                sp.dma_start(VL[:, i, :], row(d_vec[v:v + 1, :])).then_inc(S["vec_lat_loaded"], 16)
            with sp.Fori(1, 4) as c:
                w_o(c)
            wg = a["w_e_gate"][0].rearrange("e k f -> (e k) f")
            wu = a["w_e_up"][0].rearrange("e k f -> (e k) f")
            wd = a["w_e_down"][0].rearrange("e k f -> (e k) f")

            def residual_loads():
                def x_tile(t):
                    src = a["x_sample"][0][t * P:(t + 1) * P, :] if t < TT - 1 else a["x_prompt"][0]
                    sp.dma_start(R1["x_t"][:, t % 2, :], src).then_inc(S[f"xt_loaded{t % 2}"], 16)

                sp.wait_ge(phase, 5 * 4)
                x_tile(0)
                x_tile(1)
                sp.dma_start(R1["shift_lat"][:], row(d_mod[0:1, 3 * D:4 * D])).then_inc(S["shift_loaded"], 16)
                sp.dma_start(T["wr"][:], a["w_router"][0].rearrange("(k p) e -> p k e", p=P)
                             ).then_inc(S["wr_loaded"], 16)
                for t in range(2, TT):
                    sp.wait_ge(S["x2_ready"], t - 1)
                    x_tile(t)
                    if t == 2:
                        for i, v in enumerate((3, 1)):
                            sp.dma_start(R1["vec_ctx"][:, i, :], row(d_vec[v:v + 1, :])
                                         ).then_inc(S["vec_ctx_loaded"], 16)
                        sp.dma_start(R2["shift_ctx"][:], row(d_mod[1:2, 3 * D:4 * D])
                                     ).then_inc(S["vec_ctx_loaded"], 16)
                sp.wait_ge(S["h2_stored0"], 3 * 16)
                sp.wait_ge(S["h2_stored1"], 2 * 16)
                sp.wait_ge(S["logit_done"], TT)
                for v in range(2):
                    sp.dma_start(G2[:, v, :], row(d_vec[4 + v:5 + v, :])).then_inc(S["g2_loaded"], 16)

            def expert(e):
                for k in range(KT + 8):
                    u, first = Q_EXP * NRAW + e * 24 + k, isinstance(e, int) and k < 8
                    if first and k == NRAW:
                        residual_loads()
                    elif not first:
                        sp.wait_ge(lo_ready, 2 * u - 6)
                    elif k < NRAW:
                        sp.wait_ge(lo_ready, 2 * u + 2)
                    if k < KT:
                        src = [w[bass.ds(e * D + k * P, P), :] for w in (wg, wu)]
                    else:
                        src = [wd[bass.ds(e * D_EXP + (k - KT) * P, P), half_of(p)] for p in range(2)]
                    for p in range(2):
                        sp.dma_start(raw_slot(k)[:, half_of(p)], src[p]).then_inc(raw_loaded[k % 8], INC // 2)

            expert(0)
            with sp.Fori(1, NE) as e:
                expert(e)

        @block.gpsimd
        def _(pool):
            give(pool, "m_row_free", "v_free", "stage_free", "g_stage_free", "k_new_free", "o_n_free", "ye_free")

            def plain():
                pool.sem_inc(S["passed"], 1)

            def stored(done, value, free):
                pool.wait_ge(S[done], value)
                pool.sem_inc(S[free], 1)

            def flat(x):
                return x.rearrange("(r p) -> r p", p=P)

            def heads(x):
                return x.rearrange("t h e -> t (h e)")

            r2 = A["rows2"]
            loads = [(r2[0:32, :], a["conv_w"][0].rearrange("t (b p) -> (t b) p", p=P)),
                     (r2[32:40, :], flat(a["conv_b"][0])),
                     (r2[40:56, :], a["lru_br"][0].rearrange("d (b p) -> (d b) p", p=P)),
                     (r2[56:72, :], a["lru_bi"][0].rearrange("d (b p) -> (d b) p", p=P)),
                     (r2[72:88, :], a["lru_lam"][0].rearrange("d (b p) -> (d b) p", p=P)),
                     (r2[88:104, :], a["state_rnn"][0, 0].rearrange("d (b p) -> (d b) p", p=P)),
                     (r2[104:105, :], a["g_sub"])]
            loads += [(A["lamv"][0:1, i, :], a[n]) for i, n in enumerate(("lam_q1", "lam_q2", "lam_k1", "lam_k2"))]
            assert len(loads) == N_PAR
            for dst, src in loads:
                pool.dma_start(dst, src).then_inc(par_loaded, 16)
            pool.memset(A["zero"][:], 0.0).then_inc(pool_own, 1)
            pool.wait_ge(pool_own, 1)

            def mod_group(g):
                wait(pool, "m_row_ready", g)
                plain()
                pool.dma_start(A["b_row"][:], a["b_mod"][0:1, bass.ds(g * D, D)].to_broadcast([2, D])
                               ).then_inc(S["b_loaded"], 16)
                wait(pool, "m_row_ready", g + 1)
                plain()
                pool.dma_start(d_mod[:, bass.ds(g * D, D)], A["m_row"][:]).then_inc(S["m_stored"], 16)
                stored("m_stored", (g + 1) * 16, "m_row_free")

            with pool.Fori(0, 2) as g:
                mod_group(g)
            for i, (r, g) in enumerate(((0, 0), (0, 1), (1, 0), (1, 1))):
                pool.dma_start(A["rows3"][16 * i:16 * i + 16, :], flat(d_mod[r, g * D:(g + 1) * D])
                               ).then_inc(S["rows3_loaded"], 16)
            with pool.Fori(2, 6) as g:
                mod_group(g)
            change(pool, 1)
            for t in range(TT):
                pool.dma_start(d_f[t * P:(t + 1) * P, :], A["zero"][:]).then_inc(S["zero_stored"], 16)

            for i, (g, gain) in enumerate(((4, "g_pre2"), (2, "g_post1"), (5, "g_post2"))):
                for v in range(2):
                    sl = slice(32 * i + 16 * v, 32 * i + 16 * v + 16)
                    pool.dma_start(vec_rows[sl, :], flat(d_mod[v, g * D:(g + 1) * D])).then_inc(S["vrow_loaded"], 16)
                    pool.dma_start(gain_rows[sl, :], flat(a[gain][0])).then_inc(S["vrow_loaded"], 16)
            with pool.Fori(0, 2) as c:
                wait(pool, "bank_taken", TT * (c + 1))
                plain()
                pool.dma_start(d_v[:, bass.ds(c * 512, 512)].rearrange("(t p) n -> p t n", p=P), v_stage[:]
                               ).then_inc(S["v_stored"], 16)
                pool.dma_start(heads(out_v[0, 0])[:, bass.ds(c * 512, 512)], v_stage[:, TT - 1, :]
                               ).then_inc(S["v_stored"], 16)
                stored("v_stored", c * 32 + 32, "v_free")
            pool.wait_ge(S["vec_ready"], 1)
            pool.dma_start(d_vec.rearrange("v (r p) -> (v r) p", p=P), vec_rows[:]).then_inc(S["vec_stored"], 16)
            with pool.Fori(0, 8) as i:
                for j in range(4):
                    wait(pool, "in_taken", 2 * (i * 4 + j + 1))
                    plain()
                    pool.dma_start(d_proj[bass.ds((i * 4 + j) * P, P), :], stage[:, j % 2, :]
                                   ).then_inc(S["in_stored"], 16)
                    stored("in_stored", (i * 4 + j + 1) * 16, "stage_free")
            pool.wait_ge(S["vec_stored"], 16)
            pool.wait_ge(S["zero_stored"], TT * 16)
            change(pool, 2)

            for name in ("rope", "perm"):
                pool.dma_start(C[name][:], a[name]).then_inc(S["rope_loaded"], 16)

            def load_head(h):
                for name, n, ready in (("xr", 0, "xr_loaded"), ("k", 24, "k_loaded"), ("q_in", 16, "q_loaded")):
                    pool.dma_start(C[name][:], d_proj[bass.ds((h + n) * P, P), :]).then_inc(S[ready], 16)
                pool.dma_start(C["k_past"][:], heads(a["cache_k"][0, 0])[:, bass.ds(h * P, P)]
                               ).then_inc(S["kp_loaded"], 16)
                for i, w in enumerate(("lru_wr", "lru_wi")):
                    pool.dma_start(C["lru_w"][:, i::2, :], a[w][0].rearrange("d b i j -> (b i) d j")[bass.ds(h * P, P)]
                                   ).then_inc(S["lruw_loaded"], 16)
                pool.dma_start(C["gr"][:], d_proj[bass.ds((h + 8) * P, P), :]).then_inc(S["gr_loaded"], 16)

            def load_values(h):
                pool.dma_start(C["v"][:, 0, :], heads(a["cache_v"][0, 0])[:, bass.ds(h * P, P)]
                               ).then_inc(S["v_loaded"], 16)
                pool.dma_start(C["v"][:, 1:TT + 1, :], d_v[:, bass.ds(h * P, P)].rearrange("(t p) n -> p t n", p=P)
                               ).then_inc(S["v_loaded"], 16)

            def head(h, last):
                def store_gate(j):
                    wait(pool, "gate_taken", 2 * (h * 4 + j) + 2)
                    plain()
                    pool.dma_start(d_proj[bass.ds((h * 4 + 40 + j) * P, P), :], C["g_stage"][:, j % 2, :]
                                   ).then_inc(S["gate_stored"], 16)
                    stored("gate_stored", (h * 4 + j + 1) * 16, "g_stage_free")

                pool.wait_ge(S["kt_taken"], 2 * h + 2)
                plain()
                pool.dma_start(heads(out_k[0, 0])[:, bass.ds(h * P, P)], C["k_new"][:]
                               ).then_inc(S["knew_stored"], 16)
                stored("knew_stored", h * 16 + 16, "k_new_free")
                store_gate(0)
                pool.wait_ge(S["y_ready"], h + 1)
                plain()
                pool.dma_start(d_z[bass.ds(h * P, P), :], L["h_f"][:]).then_inc(S["y_stored"], 16)
                if not last:
                    load_head(h + 1)
                store_gate(1)
                store_gate(2)
                if not last:
                    pool.wait_ge(S["av_done"], h + 1)
                    plain()
                    load_values(h + 1)
                store_gate(3)
                wait(pool, "o_ready", 2 * h + 2)
                plain()
                pool.dma_start(d_z[bass.ds((h + 8) * P, P), :], C["o_n"][:]).then_inc(S["o_stored"], 16)
                stored("o_stored", h * 16 + 16, "o_n_free")

            load_head(0)
            load_values(0)
            with pool.Fori(0, NH - 1) as h:
                head(h, False)
            head(NH - 1, True)
            pool.wait_ge(S["y_stored"], NH * 16)
            change(pool, 3)

            with pool.Fori(0, 4) as i:
                for j in range(4):
                    wait(pool, "mix_done", i * 4 + j - 1)
                    plain()
                    for s in range(2):
                        pool.dma_start(G["gate"][:, j % 2, s, :], d_proj[bass.ds((i * 4 + 40 + s * KT + j) * P, P), :]
                                       ).then_inc(S[f"g_loaded{j % 2}"], 16)
            change(pool, 4)
            change(pool, 5)

            for t in range(TT):
                pool.wait_ge(S["h2_ready"], t + 1)
                pool.dma_start(d_h2[t * P:(t + 1) * P, :], R2["h2"][:, t % 2, :]).then_inc(S[f"h2_stored{t % 2}"], 16)
            pool.wait_ge(S["h2_stored0"], 3 * 16)
            pool.wait_ge(S["h2_stored1"], 2 * 16)
            change(pool, 6)

            def gather(e):
                pool.wait_ge(S["idx_ready"], e + 1)
                plain()
                pool.indirect_dma_start(E["xs"][0:CAP, :], None, d_h2,
                                        bass.IndirectOffsetOnAxis(T["idx_e"][0:CAP, 0:1], 0)
                                        ).then_inc(S["gathered"], 16)

            def scatter(e):
                wait(pool, "ye_ready", 2 * e + 2)
                plain()
                pool.indirect_dma_start(d_f, bass.IndirectOffsetOnAxis(T["sidx"][0:CAP, 0:1], 0), E["ye"][0:CAP, :],
                                        None, compute_op=ALU.add).then_inc(S["scattered"], 16)
                stored("scattered", (e + 1) * 16, "ye_free")

            gather(0)
            with pool.Fori(0, NE - 1) as e:
                gather(e + 1)
                scatter(e)
            scatter(NE - 1)
            change(pool, 7)

        @block.scalar
        def _(act):
            give(act, "in_taken", "gate_taken", "pdT_taken")
            own = Own(act, act_own)
            r1 = A["rows1"]
            for dst, src in ((r1[0:16, :], a["c"][0]), (r1[16:32, :], a["c_ctx"]), (r1[32:48, :], a["g_pre1"][0])):
                act.dma_start(dst, src.rearrange("(r p) -> r p", p=P)).then_inc(S["c_loaded"], 16)
            act.dma_start(ident[:], a["ident"]).then_inc(S["c_loaded"], 16)
            split_hi(act, Q_MOD, 0)
            act.wait_ge(S["cols_ready"], 1)
            act.activation(A["sc"][:], A["cols1"][:, 0:32], ACT.Silu).then_inc(S["c_act"], 1)
            act.wait_ge(S["c_act"], 1)
            act.activation(c_hi[:], A["sc"][:].rearrange("p (v k) -> p k v", v=2), ACT.Copy).then_inc(S["c_act"], 1)

            def square(t):
                if t == 0:
                    act.wait_ge(x_lat_loaded, (TT - 1) * 16)
                    act.wait_ge(S["const_set"], 1)
                if t == TT - 1:
                    act.wait_ge(x_ctx_loaded, 16)
                own.settle()
                own.done(act.activation(A["junk0"][:], x_in[:, t, :], ACT.Square, accum_out=stats[:, t:t + 1]))
                own.settle()
                act.activation(stats[:, 8 + t:9 + t], stats[:, t:t + 1], ACT.Sqrt, bias=eps_col, scale=1.0 / D
                               ).then_inc(S["sqrt_x"], 1)

            def take_x(t):
                for kq in (0, 2):
                    act.wait_ge(S["x_turned"], 4 * t + kq + 1)
                    act.activation(xT[:, 4 * kq:4 * kq + 4, t * P:(t + 1) * P],
                                   ps[:, 4 + kq, :].rearrange("p (k n) -> p k n", k=4), ACT.Copy
                                   ).then_inc(S["xt_act"], 1)

            def tokens(k):
                for v, s in ((0, slice(0, N_LAT)), (1, slice(N_LAT, N_TOK))):
                    own.done(act.activation(xT[:, k, s], xT[:, k, s], ACT.Identity, scale=A["A1"][:, v, k:k + 1],
                                            bias=A["cols3"][:, 32 * v + k:32 * v + k + 1]))
                own.settle()
                act.activation(hi[:, k, :], xT[:, k, :], ACT.Copy).then_inc(S["tok_hi"], 1)

            for k in range(KT):
                split_hi(act, Q_MOD, k + 1, fine=True)
                if k >= 4 and k % 2 == 0 and (k - 4) // 2 < TT:
                    t = (k - 4) // 2
                    if t < TT - 1:
                        act.dma_start(x_in[:, t, :], a["x_sample"][0][t * P:(t + 1) * P, :]).then_inc(x_lat_loaded, 16)
                    else:
                        act.dma_start(x_in[:, t, :], a["x_prompt"][0]).then_inc(x_ctx_loaded, 16)
            act.wait_ge(S["small_dve"], 1)
            act.activation(A["lams"][0:1, 2:4], A["lams"][0:1, 0:2], ACT.Exp).then_inc(S["small_act"], 1)
            act.wait_ge(S["small_dve"], 2)
            act.activation(A["sp_b"][:], A["sp_a"][:], ACT.Exp, scale=-1.0).then_inc(S["small_act"], 1)
            for k in range(KT):
                split_hi(act, Q_MOD + 4, k + 1, fine=True)
                if k % 3 == 0 and k < 3 * TT:
                    square(k // 3)
                if k % 3 == 2 and k // 3 < TT:
                    take_x(k // 3)
            for g in range(2, 6):
                for k in range(KT):
                    split_hi(act, Q_MOD + g * 4, k + 1, fine=True)
                    if g == 2 and k == 11:
                        act.wait_ge(S["a1_ready"], 1)
                    if (g == 2 and k >= 12) or (g > 2 and k % 4 == 3):
                        tokens((g - 2) * 4 + (k - 12 if g == 2 else k // 4))
            change(act, 1)

            with act.Fori(0, 2) as c:
                for kq in range(4):
                    split_hi(act, Q_V + c, kq + 1)
            with act.Fori(0, 8) as i:
                for j in range(4):
                    split_hi(act, Q_IN + i, j + 1)
                    act.wait_ge(S["in_a_done"], i * 4 + j + 1)
                    wait(act, "stage_free", i * 4 + j - 1)
                    act.activation(stage[:, j % 2, 0:HALF], ps[:, 5, 0:HALF], ACT.Copy).then_inc(S["in_taken"], 1)
                    act.wait_ge(halves_used, used(i * 4 + j + Q_IN * 4 + 1))
                    act.activation(stage[:, j % 2, HALF:N_TOK], ps[:, 6, 0:HALF], ACT.Copy
                                   ).then_inc(S["in_taken"], 1)
            change(act, 2)

            att = C["att"]
            with act.Fori(0, NH) as h:
                def take(j, half):
                    if half == 0:
                        act.wait_ge(S["gate_a_done"], h * 4 + j + 1)
                        wait(act, "g_stage_free", h * 4 + j - 1)
                    else:
                        act.wait_ge(halves_used, used(h * 4 + Q_GATE * 4 + j + 1))
                    act.activation(C["g_stage"][:, j % 2, half * HALF:(half + 1) * HALF], ps[:, 5 + half, 0:HALF],
                                   ACT.Copy).then_inc(S["gate_taken"], 1)

                def lru_gates(d):
                    act.wait_ge(S["lru_mm"], h * 2 + d + 1)
                    if d:
                        act.wait_ge(S["lru_b"], h * 2 + d)
                    for i, dst in ((0, "lr"), (1, "li")):
                        act.activation(halves(L[dst][:]), ps[:, 2 * i:2 * i + 2, 0:HALF], ACT.Sigmoid,
                                       bias=C["prm"][:, (BR, BI)[i] + d:(BR, BI)[i] + d + 1]).then_inc(S["lru_sig"], 1)
                    if d:
                        act.wait_ge(S["lru_scan"], h * 2 + d)
                    act.wait_ge(S["lru_sig"], h * 4 + 2 * d + 2)
                    act.activation(L["la"][:], L["lr"][:], ACT.Exp, scale=C["prm"][:, NEG + d:NEG + d + 1]
                                   ).then_inc(S["lru_at"], 1)
                    act.activation(L["lt"][:], L["lr"][:], ACT.Tanh, scale=C["prm"][:, LAM_ + d:LAM_ + d + 1]
                                   ).then_inc(S["lru_at"], 1)

                def lru_root(d):
                    act.wait_ge(S["lru_q"], h * 2 + d + 1)
                    act.activation(L["lt"][:], L["ld"][:], ACT.Sqrt).then_inc(S["lru_sqrt"], 1)

                def exps(qt):
                    act.wait_ge(S["score_max"], h * TT + qt + 1)
                    if qt == 0:
                        act.wait_ge(S["y_ready"], h + 1)
                    if qt >= 2:
                        act.wait_ge(S["pdT_done"], h * TT + qt - 1)
                    for c in range(2):
                        if qt < TT - 1:
                            dst, src = halves(C["probs"][:, qt % 2, c, :]), ps[:, 2 * c:2 * c + 2, 0:HALF]
                        else:
                            dst, src = C["probs"][:, qt % 2, c, 0:P], ps[:, 2 * c, 0:P]
                        i = 4 * (qt % 2) + c
                        act.activation(dst, src, ACT.Exp, scale=ATT_SCALE, bias=att[:, i:i + 1],
                                       accum_out=att[:, 8 + i:9 + i]).then_inc(S["score_exp"], 1)

                def take_T(qt):
                    act.wait_ge(S["pdT_done"], h * TT + qt + 1)
                    if qt == 0:
                        act.wait_ge(S["y_stored"], h * 16 + 16)
                    if qt < TT - 1:
                        act.activation(C["pT"][:, 0:4, qt * P:(qt + 1) * P],
                                       ps[:, 4, :].rearrange("p (k n) -> p k n", k=4), ACT.Copy)
                        act.activation(C["pT"][:, 4, qt * P:(qt + 1) * P], ps[:, 7, 0:P], ACT.Copy
                                       ).then_inc(S["pdT_taken"], 1)
                    else:
                        act.activation(C["pT_ctx"][:], ps[:, 4, 0:P], ACT.Copy).then_inc(S["pdT_taken"], 1)

                split_hi(act, Q_GATE + h, 1)
                act.wait_ge(S["prm_set"], h + 1)
                take(0, 0)
                take(0, 1)
                lru_gates(0)
                lru_root(0)
                split_hi(act, Q_GATE + h, 2)
                take(1, 0)
                lru_gates(1)
                lru_root(1)
                act.wait_ge(S["gr_loaded"], h * 16 + 16)
                act.activation(L["gel"][:], C["gr"][:], ACT.Gelu_apprx_tanh).then_inc(S["gelu_done"], 1)
                take(1, 1)
                exps(0)
                split_hi(act, Q_GATE + h, 3)
                exps(1)
                take(2, 0)
                take_T(0)
                exps(2)
                take_T(1)
                exps(3)
                take(2, 1)
                take_T(2)
                exps(4)
                split_hi(act, Q_GATE + h, 4)
                take_T(3)
                take_T(4)
                take(3, 0)
                act.wait_ge(S["av_done"], h + 1)
                for b, s in ((0, slice(0, N_LAT)), (1, slice(N_LAT, N_TOK))):
                    last = act.activation(C["probs"][:, 0, 0, s], ps[:, b, 0:s.stop - s.start], ACT.Square)
                last.then_inc(S["o_sq"], 1)
                take(3, 1)
                act.wait_ge(S["ms_done"], h + 1)
                for b, s in ((2, slice(0, N_LAT)), (3, slice(N_LAT, N_TOK))):
                    last = act.activation(C["rsd"][:, s], ps[:, b, 0:s.stop - s.start], ACT.Sqrt, bias=eps_col)
                last.then_inc(S["ms_sqrt"], 1)
            def branch(k):
                brings = {0: (S["z_loaded0"], 16), 4: (S["z_loaded1"], 16), NB: (S["z_loaded0"], 32),
                          KT - 1: (S["z_loaded1"], 32)}
                if k in brings:
                    act.wait_ge(*brings[k])
                act.activation(hi[:, k, :], zT[:, k, :], ACT.Copy).then_inc(S["split_in_hi"], 1)

            for k in range(KT - 1):
                branch(k)
            change(act, 3)
            branch(KT - 1)
            with act.Fori(0, 4) as i:
                for j in range(4):
                    act.wait_ge(S[f"g_loaded{j % 2}"], (i * 2 + j // 2) * 32 + 32)
                    act.activation(G["gate"][:, j % 2, :, :], G["gate"][:, j % 2, :, :], ACT.Sigmoid
                                   ).then_inc(S["g_sig"], 1)
                    split_hi(act, Q_AB + i, j + 1)
            change(act, 4)

            for k in range(KT):
                act.activation(hi[:, k, :], mix[:, k, :], ACT.Copy).then_inc(S["split_in_hi"], 1)
            for c in range(4):
                for kq in range(4):
                    split_hi(act, Q_O + c, kq + 1)
                for t in range(TT):
                    wait(act, "o_taken", c * TT + t + 1)
                    own.settle()
                    own.done(act.activation(junk_o[:], t_out[:, t, c * 512:(c + 1) * 512], ACT.Square,
                                            accum_out=stats[:, 16 + 4 * t + c:17 + 4 * t + c]))
            change(act, 5)

            act.wait_ge(S["rs1_sum"], 1)
            act.activation(stats[:, 40:40 + TT], stats[:, 40:40 + TT], ACT.Sqrt, bias=eps_col, scale=1.0 / D
                           ).then_inc(S["rs1_sqrt"], 1)

            def square(t):
                act.wait_ge(S["x2_ready"], t + 1)
                if t:
                    own.settle()
                own.done(act.activation(R2["junk1"][:], t_out[:, t, :], ACT.Square, accum_out=stats[:, 48 + t:49 + t]))
                own.settle()
                act.activation(stats[:, 48 + t:49 + t], stats[:, 48 + t:49 + t], ACT.Sqrt, bias=eps_col, scale=1.0 / D
                               ).then_inc(S["x2_sqrt"], 1)

            def take_h2(t):
                act.wait_ge(S["h2T_done"], t + 1)
                if t:
                    act.wait_ge(S["logit_done"], t)
                act.activation(R2["h2T"][:].rearrange("p (b k) n -> p b (k n)", b=4), ps[:, 0:4, :], ACT.Copy
                               ).then_inc(S["h2T_taken"], 1)

            def exp_logits(t):
                act.wait_ge(S["logit_max"], t + 1)
                act.activation(T["aff"][:], ps[:, 4 + 2 * (t % 2), 0:NE], ACT.Exp, bias=T["sm"][:, 1:2],
                               accum_out=T["sm"][:, 2:3]).then_inc(S["logit_exp"], 1)

            square(0)
            for t in range(TT + 2):
                if t + 1 < TT:
                    square(t + 1)
                if t < TT:
                    take_h2(t)
                if 1 <= t <= TT:
                    exp_logits(t - 1)
            change(act, 6)

            def take_xs(e):
                act.wait_ge(S["xsT_done"], e + 1)
                act.activation(xs_hi[:].rearrange("p (b k) n -> p b (k n)", b=4), ps[:, 0:4, 0:4 * CAP], ACT.Copy
                               ).then_inc(S["xs_hi_done"], 1)

            def expert(e, last):
                quad = Q_EXP + e * 6
                for k in range(KT):
                    exp_split_hi(act, e, k + 1)
                act.wait_ge(halves_used, used((quad + 4) * 4) - 1)
                act.activation(E["hid"][0:CAP, :].rearrange("p (b n) -> p b n", b=2), ps[0:CAP, 0:2, :], ACT.Silu
                               ).then_inc(S["silu_done"], 1)
                act.wait_ge(S["hidT_done"], e + 1)
                act.activation(hid_hi[:].rearrange("p (b k) n -> p b (k n)", b=2), ps[:, 4:6, 0:4 * CAP], ACT.Copy
                               ).then_inc(S["hidT_hi"], 1)
                for k in range(8):
                    if not (last and k == 7):
                        exp_split_hi(act, e, KT + k + 1)
                    if k == 2 and not last:
                        take_xs(e + 1)
                act.wait_ge(halves_used, used((quad + 6) * 4))
                act.wait_ge(S["val_set"], e + 1)
                act.activation(E["ye"][0:CAP, 0:1024].rearrange("p (b n) -> p b n", b=2), ps[0:CAP, 4:6, :],
                               ACT.Identity, scale=T["val_e"][0:CAP, :]).then_inc(S["ye_ready"], 1)

            take_xs(0)
            with act.Fori(0, NE - 1) as e:
                expert(e, False)
            expert(NE - 1, True)
            change(act, 7)

            for t in range(TT):
                act.dma_start(Z["f"][:, t, :], d_f[t * P:(t + 1) * P, :]).then_inc(S[f"f_loaded{min(t, 2)}"], 16)
            for t in range(TT):
                act.wait_ge(S[f"f_loaded{min(t, 2)}"], 16 if t < 2 else 48)
                if t:
                    own.settle()
                own.done(act.activation(junk2[:], Z["f"][:, t, :], ACT.Square, accum_out=stats[:, t:t + 1]))
                own.settle()
                act.activation(stats[:, 8 + t:9 + t], stats[:, t:t + 1], ACT.Sqrt, bias=eps_col, scale=1.0 / D
                               ).then_inc(S["f_sqrt"], 1)
            for t in range(TT):
                act.wait_ge(S["y_done"], t + 1)
                dst = out_lat[0, t * P:(t + 1) * P, :] if t < TT - 1 else out_ctx[0]
                act.dma_start(dst, Z["f"][:, t, :]).then_inc(S["y_out"], 16)
            act.wait_ge(S["state_row"], 1)
            act.dma_start(out_state[0, 0].rearrange("d (b p) -> (d b) p", p=P), state_rows[:]
                          ).then_inc(S["state_stored"], 16)
            act.wait_ge(S["y_out"], TT * 16)
            act.wait_ge(S["state_stored"], 16)

        @block.vector
        def _(dve):
            give(dve, "m_row_ready", "bank_taken", "o_ready", "mix_done", "o_taken", "ye_ready")
            dve.sem_inc(lo_ready, 2 * NRAW)
            own = Own(dve, dve_own)
            TS, TTn, STT = dve.tensor_scalar, dve.tensor_tensor, dve.scalar_tensor_tensor

            dve.memset(eps_col, EPS)
            dve.memset(mean_mat[:], 1.0 / P)
            dve.memset(A["ones_row"][:], 1.0).then_inc(S["const_set"], 1)
            dve.wait_ge(S["rows_turned"], 1)
            dve.tensor_copy(A["cols1"][:], ps[:, 7, 0:48]).then_inc(S["cols_ready"], 1)
            dve.wait_ge(S["c_act"], 2)
            TTn(c_lo[:], A["sc"][:].rearrange("p (v k) -> p k v", v=2), c_hi[:].bitcast(F32), ALU.subtract
                ).then_inc(S["c_ready"], 1)
            split_lo(dve, Q_MOD, 0)

            def norm_diagonal(t):
                dve.wait_ge(S["sqrt_x"], t + 1)
                own.done(dve.reciprocal(stats[:, 16 + t:17 + t], stats[:, 8 + t:9 + t]))
                own.settle()
                TS(A["diag"][:, t % 2, :], ident[:], stats[:, 16 + t:17 + t], None, ALU.mult).then_inc(S["xn_ready"], 1)

            def take_x(t):
                for kq in (1, 3):
                    dve.wait_ge(S["x_turned"], 4 * t + kq + 1)
                    dve.tensor_copy(xT[:, 4 * kq:4 * kq + 4, t * P:(t + 1) * P],
                                    ps[:, 4 + kq, :].rearrange("p (k n) -> p k n", k=4)).then_inc(S["xt_dve"], 1)

            def first_vectors():
                dve.wait_ge(S["rows3_turned"], 1)
                own.done(dve.tensor_copy(A["cols3"][:], ps[:, 7, 0:64]))
                own.settle()
                for v in range(2):
                    last = STT(A["A1"][:, v, :], A["cols3"][:, 32 * v + 16:32 * v + 32], 1.0, A["cols1"][:, 32:48],
                               ALU.add, ALU.mult)
                    own.done(last) if v == 0 else last.then_inc(S["a1_ready"], 1)

            def tokens(k):
                dve.wait_ge(S["tok_hi"], k + 1)
                TTn(lo[:, k, :], xT[:, k, :], hi[:, k, :].bitcast(F32), ALU.subtract).then_inc(S["tok_lo"], 1)

            def mod_rows(g):
                dve.wait_ge(S["b_loaded"], g * 16 + 16)
                wait(dve, "m_row_free", g)
                dve.wait_ge(halves_used, used((Q_MOD + g * 4 + 4) * 4))
                TTn(A["m_row"][:].rearrange("p (b n) -> p b n", b=4), ps[0:2, 0:4, :],
                    A["b_row"][:].rearrange("p (b n) -> p b n", b=4), ALU.add).then_inc(S["m_row_ready"], 1)

            for k in range(KT):
                split_lo(dve, Q_MOD, k + 1, fine=True)
            dve.wait_ge(S["rows_turned"], 2)
            dve.tensor_copy(A["cols2"][:], ps[:, 7, 128:233]).then_inc(S["cols_ready"], 1)
            dve.wait_ge(par_loaded, N_PAR * 16)
            own.done(TTn(A["lamp"][:], A["lamv"][:, 0:2, :], A["lamv"][:, 2:4, :], ALU.mult))
            own.settle()
            dve.tensor_reduce(A["lams"][0:1, 0:2], A["lamp"][:], AX.X, ALU.add).then_inc(S["small_dve"], 1)
            dve.wait_ge(S["small_act"], 1)
            own.done(TTn(A["lams"][0:1, 4:5], A["lams"][0:1, 2:3], A["lams"][0:1, 3:4], ALU.subtract))
            own.settle()
            TS(A["lams"][0:1, 5:6], A["lams"][0:1, 4:5], LAM_INIT, None, ALU.add).then_inc(S["lam_val"], 1)
            lam16, sa, sb_, sc_, sd = A["cols2"][:, 72:88], A["sp_a"][:], A["sp_b"][:], A["sp_c"][:], A["sp_d"][:]
            dve.wait_ge(S["cols_ready"], 2)
            own.done(TS(sc_, lam16, -1.0, None, ALU.mult))
            own.settle()
            TTn(sa, lam16, sc_, ALU.max).then_inc(S["small_dve"], 1)
            dve.wait_ge(S["small_act"], 2)
            own.done(TS(sd, sb_, 2.0, None, ALU.add))
            own.settle()
            own.done(dve.reciprocal(sa, sd))
            own.settle()
            own.done(TTn(sb_, sb_, sa, ALU.mult))
            own.settle()
            own.done(TTn(sa, sb_, sb_, ALU.mult))
            own.settle()
            own.done(TS(sd, sa, 1.0 / 15, None, ALU.mult))
            own.settle()
            for n in (13, 11, 9, 7, 5, 3):
                own.done(STT(sd, sd, 1.0 / n, sa, ALU.add, ALU.mult))
                own.settle()
            own.done(STT(sd, sd, 1.0, sb_, ALU.add, ALU.mult))
            own.done(TS(sc_, sc_, 0.0, None, ALU.max))
            own.settle()
            own.done(STT(sd, sd, 2.0, sc_, ALU.mult, ALU.add))
            own.done(dve.tensor_copy(prm_all[:, :, 0:13].rearrange("p b m -> p m b"),
                                     A["cols2"][:, 0:104].rearrange("p (m b) -> p m b", b=NB)))
            own.settle()
            sdv = sd.rearrange("p (m b) -> p m b", b=NB)
            own.done(TS(prm_all[:, :, LAM_:LAM_ + 2].rearrange("p b m -> p m b"), sdv, 8.0, None, ALU.mult))
            own.done(TS(prm_all[:, :, NEG:NEG + 2].rearrange("p b m -> p m b"), sdv, -8.0, None, ALU.mult))
            own.done(TS(gsub_col, A["cols2"][:, 104:105], 1.0 - LAM_INIT, None, ALU.mult))
            dve.wait_ge(S["lam_spread"], 1)
            own.done(dve.tensor_copy(lam_col, ps[:, 6, 0:1]))
            mod_rows(0)
            for k in range(KT):
                split_lo(dve, Q_MOD + 4, k + 1, fine=True)
                if k % 3 == 0 and k < 3 * TT:
                    norm_diagonal(k // 3)
                if k % 3 == 2 and k // 3 < TT:
                    take_x(k // 3)
            mod_rows(1)
            for g in range(2, 6):
                for k in range(KT):
                    split_lo(dve, Q_MOD + g * 4, k + 1, fine=True)
                    if g == 2 and k == 10:
                        first_vectors()
                    if k == KT - 1:
                        mod_rows(g)
                    if (g == 2 and k >= 12) or (g > 2 and k % 4 == 3):
                        tokens((g - 2) * 4 + (k - 12 if g == 2 else k // 4))
            change(dve, 1)

            with dve.Fori(0, 2) as c:
                for kq in range(4):
                    split_lo(dve, Q_V + c, kq + 1)
                wait(dve, "v_free", c)
                for t in range(TT):
                    if t < TT - 1:
                        dve.wait_ge(S["bank_done"], c * (TT - 1) + t + 1)
                    else:
                        dve.wait_ge(halves_used, used((Q_V + c + 1) * 4))
                    dve.tensor_copy(v_stage[:, t, :], ps[:, t, :]).then_inc(S["bank_taken"], 1)
            dve.wait_ge(S["vrow_loaded"], 12 * 16)
            own.done(TS(vec_rows[0:32, :], vec_rows[0:32, :], 1.0, None, ALU.add))
            own.settle()
            TTn(vec_rows[:], vec_rows[:], gain_rows[:], ALU.mult).then_inc(S["vec_ready"], 1)
            with dve.Fori(0, 8) as i:
                for j in range(4):
                    split_lo(dve, Q_IN + i, j + 1)
            change(dve, 2)

            prm, att = C["prm"], C["att"]
            with dve.Fori(0, NH) as h:
                own.enter(h, PER_HEAD)
                split_lo(dve, Q_GATE + h, 1)
                dve.tensor_copy(prm[:, 0:NPRM], prm_all[:, bass.ds(h, 1), :].rearrange("p o m -> p (o m)")
                                ).then_inc(S["prm_set"], 1)
                dve.wait_ge(S["prm_set"], h + 1)
                dve.wait_ge(S["xr_loaded"], h * 16 + 16)
                xr, xc = C["xr"], C["xc"]
                spans = ((0, N_LAT), (N_LAT, N_TOK))
                for b, e in spans:
                    own.done(TS(xc[:, b:e], xr[:, b:e], prm[:, CW + 2:CW + 3], prm[:, CB:CB + 1], ALU.mult, ALU.add))
                for tap, off in ((0, -2), (1, -1), (3, 1)):
                    own.settle()
                    for b, e in spans:
                        d0, d1 = (b - off, e) if off < 0 else (b, e - off)
                        last = STT(xc[:, d0:d1], xr[:, d0 + off:d1 + off], prm[:, CW + tap:CW + tap + 1],
                                   xc[:, d0:d1], ALU.mult, ALU.add)
                        if tap == 3 and e == N_TOK:
                            last.then_inc(S["xc_ready"], 1)
                        else:
                            own.done(last)
                dve.wait_ge(S["kt_done"], h + 1)
                wait(dve, "k_new_free", h)
                dve.tensor_copy(C["k_all"][:, 0:PAST], ps[:, 4, 0:P]).then_inc(S["kt_taken"], 1)
                dve.tensor_copy(C["k_new"][:], ps[:, 7, 0:P]).then_inc(S["kt_taken"], 1)
                dve.wait_ge(S["rope_loaded"], 32)

                def rotate(i, x, dst):
                    dve.wait_ge(S["rot_done"], h * 2 + i + 1)
                    own.done(TTn(x[:, 0:N_LAT], x[:, 0:N_LAT], C["rope"][:, 0, :], ALU.mult))
                    TTn(C["turned"][:], ps[:, i, :], C["rope"][:, 1, :], ALU.mult).then_inc(S["rot_read"], 1)
                    dve.wait_ge(S["rot_read"], h * 2 + i + 1)
                    own.settle()
                    dve.tensor_copy(dst[:, N_LAT:], x[:, N_LAT:]).then_inc(S["qk_ready"], 1)
                    TTn(dst[:, 0:N_LAT], x[:, 0:N_LAT], C["turned"][:], ALU.add).then_inc(S["qk_ready"], 1)

                rotate(0, C["k"], C["k_all"][:, PAST:])
                dve.wait_ge(S["qk_ready"], h * 4 + 2)
                rotate(1, C["q_in"], C["q"])

                def lru(d):
                    dst = L[("h_f", "h_b")[d]]
                    dve.wait_ge(S["lru_at"], h * 4 + 2 * d + 2)
                    own.done(TTn(L["ld"][:], L["la"][:], L["la"][:], ALU.mult))
                    own.settle()
                    STT(L["ld"][:], L["ld"][:], 1.0, L["lt"][:], ALU.add, ALU.mult).then_inc(S["lru_q"], 1)
                    own.done(TTn(L["li"][:], L["li"][:], xc[:], ALU.mult))
                    own.settle()
                    dve.wait_ge(S["lru_sqrt"], h * 2 + d + 1)
                    TTn(L["ld"][:], L["li"][:], L["lt"][:], ALU.mult).then_inc(S["lru_b"], 1)
                    dve.wait_ge(S["lru_b"], h * 2 + d + 1)
                    for n, (b, e) in enumerate(spans):
                        init = prm[:, H0 + d:H0 + d + 1] if n == 0 else 0.0
                        sl = slice(b, e) if d == 0 else slice(e - 1, b - 1 if b else None, -1)
                        last = dve.tensor_tensor_scan(dst[:, sl], L["la"][:, sl], L["ld"][:, sl], init, ALU.mult, ALU.add)
                        own.done(last) if n == 0 else last.then_inc(S["lru_scan"], 1)
                    dve.wait_ge(S["lru_scan"], h * 2 + d + 1)
                    end = N_TOK - 1 if d == 0 else N_LAT
                    own.done(dve.tensor_copy(state_col[:, bass.ds(h + d * NB, 1)], dst[:, end:end + 1]))

                lru(0)
                split_lo(dve, Q_GATE + h, 2)
                lru(1)
                own.done(TTn(L["h_f"][:], L["h_f"][:], L["h_b"][:], ALU.add))
                own.settle()
                dve.wait_ge(S["gelu_done"], h + 1)
                TTn(L["h_f"][:], L["h_f"][:], L["gel"][:], ALU.mult).then_inc(S["y_ready"], 1)

                def row_max(qt):
                    dve.wait_ge(S["score_done"], h * TT + qt + 1)
                    for c in range(2):
                        src = ps[:, 2 * c:2 * c + 2, 0:HALF] if qt < TT - 1 else ps[:, 2 * c, 0:P]
                        own.done(dve.tensor_reduce(att[:, 16 + c:17 + c], src, AX.XY if qt < TT - 1 else AX.X, ALU.max))
                    own.settle()
                    i = 4 * (qt % 2)
                    TS(att[:, i:i + 2], att[:, 16:18], -ATT_SCALE, None, ALU.mult).then_inc(S["score_max"], 1)

                def differ(qt):
                    dve.wait_ge(S["score_exp"], h * 2 * TT + 2 * qt + 2)
                    i = 8 + 4 * (qt % 2)
                    n = NKEY if qt < TT - 1 else P
                    p1, p2 = C["probs"][:, qt % 2, 0, 0:n], C["probs"][:, qt % 2, 1, 0:n]
                    own.done(dve.reciprocal(att[:, 20:22], att[:, i:i + 2]))
                    own.settle()
                    own.done(TTn(att[:, 22:23], att[:, 21:22], lam_col, ALU.mult))
                    own.settle()
                    own.done(TS(p2, p2, att[:, 22:23], None, ALU.mult))
                    own.settle()
                    STT(p1, p1, att[:, 20:21], p2, ALU.mult, ALU.subtract).then_inc(S["pd_ready"], 1)

                row_max(0)
                differ(0)
                split_lo(dve, Q_GATE + h, 3)
                for qt in range(1, TT):
                    row_max(qt)
                    differ(qt)
                split_lo(dve, Q_GATE + h, 4)
                dve.wait_ge(S["ms_sqrt"], h + 1)
                own.done(dve.reciprocal(C["rsd"][:], C["rsd"][:]))
                own.settle()
                wait(dve, "o_n_free", h)
                for b, s in ((0, slice(0, N_LAT)), (1, slice(N_LAT, N_TOK))):
                    STT(C["o_n"][:, s], ps[:, b, 0:s.stop - s.start], gsub_col, C["rsd"][:, s], ALU.mult, ALU.mult
                        ).then_inc(S["o_ready"], 1)
            own.leave(NH)
            def branch(k):
                dve.wait_ge(S["split_in_hi"], k + 1)
                TTn(lo[:, k, :], zT[:, k, :], hi[:, k, :].bitcast(F32), ALU.subtract).then_inc(S["split_in_lo"], 1)

            for k in range(KT - 1):
                branch(k)
            change(dve, 3)
            branch(KT - 1)
            with dve.Fori(0, 4) as i:
                own.enter(i, 8)
                for j in range(4):
                    split_lo(dve, Q_AB + i, j + 1)
                    b = 4 * (j % 2)
                    dve.wait_ge(S["g_sig"], i * 4 + j + 1)
                    dve.wait_ge(S["ab_a"], i * 4 + j + 1)
                    m = mix[:, bass.ds(i * 4 + j, 1), :].rearrange("p o n -> p (o n)")
                    own.done(TTn(halves(m), ps[:, b:b + 2, 0:HALF], halves(G["gate"][:, j % 2, 0, :]), ALU.mult))
                    wait(dve, "mix_done", i * 4 + j)
                    dve.wait_ge(halves_used, used(i * 4 + Q_AB * 4 + j + 1))
                    own.done(TTn(halves(G["mix_b"][:]), ps[:, b + 2:b + 4, 0:HALF],
                                 halves(G["gate"][:, j % 2, 1, :]), ALU.mult))
                    own.settle()
                    TTn(m, m, G["mix_b"][:], ALU.add).then_inc(S["mix_done"], 1)
            own.leave(4)
            change(dve, 4)

            for k in range(KT):
                dve.wait_ge(S["split_in_hi"], KT + k + 1)
                TTn(lo[:, k, :], mix[:, k, :], hi[:, k, :].bitcast(F32), ALU.subtract).then_inc(S["split_in_lo"], 1)
            for c in range(4):
                for kq in range(4):
                    split_lo(dve, Q_O + c, kq + 1)
                for t in range(TT):
                    o_bank_wait(dve, c, t)
                    dve.tensor_copy(t_out[:, t, c * 512:(c + 1) * 512], ps[:, t, :]).then_inc(S["o_taken"], 1)
            change(dve, 5)

            dve.tensor_reduce(stats[:, 40:40 + TT], stats[:, 16:36].rearrange("p (t c) -> p t c", c=4), AX.X, ALU.add
                              ).then_inc(S["rs1_sum"], 1)
            dve.wait_ge(S["rs1_sqrt"], 1)
            own.done(dve.reciprocal(stats[:, 40:40 + TT], stats[:, 40:40 + TT]))
            sm, aff = T["sm"], T["aff"]

            def residual(t):
                dve.wait_ge(*((S["vec_lat_loaded"], 32) if t < TT - 1 else (S["vec_ctx_loaded"], 48)))
                gate = VL[:, 0, :] if t < TT - 1 else R1["vec_ctx"][:, 0, :]
                x = t_out[:, t, :]
                own.settle()
                own.done(STT(x, x, stats[:, 40 + t:41 + t], gate, ALU.mult, ALU.mult))
                own.settle()
                dve.wait_ge(S[f"xt_loaded{t % 2}"], (t // 2 + 1) * 16)
                TTn(x, x, R1["x_t"][:, t % 2, :], ALU.add).then_inc(S["x2_ready"], 1)

            def second_norm(t):
                dve.wait_ge(S["x2_sqrt"], t + 1)
                own.done(dve.reciprocal(stats[:, 56 + t:57 + t], stats[:, 48 + t:49 + t]))
                own.settle()
                if t >= 2:
                    dve.wait_ge(S[f"h2_stored{t % 2}"], t // 2 * 16)
                    dve.wait_ge(S["h2T_done"], t - 1)
                dve.wait_ge(S["shift_loaded"], 16)
                scale, shift = ((VL[:, 1, :], R1["shift_lat"][:]) if t < TT - 1 else
                                (R1["vec_ctx"][:, 1, :], R2["shift_ctx"][:]))
                h2 = R2["h2"][:, t % 2, :]
                own.done(STT(h2, t_out[:, t, :], stats[:, 56 + t:57 + t], scale, ALU.mult, ALU.mult))
                own.settle()
                TTn(h2, h2, shift, ALU.add).then_inc(S["h2_ready"], 1)

            def affinities(t):
                dve.wait_ge(S["logit_done"], t + 1)
                own.done(dve.tensor_reduce(sm[:, 0:1], ps[:, 4 + 2 * (t % 2), 0:NE], AX.X, ALU.max))
                own.settle()
                TS(sm[:, 1:2], sm[:, 0:1], -1.0, None, ALU.mult).then_inc(S["logit_max"], 1)
                dve.wait_ge(S["logit_exp"], t + 1)
                own.done(dve.reciprocal(sm[:, 3:4], sm[:, 2:3]))
                own.settle()
                TS(aff[:], aff[:], sm[:, 3:4], None, ALU.mult).then_inc(S["aff_ready"], 1)
                dve.wait_ge(S["affT_done"], t + 1)
                dve.tensor_copy(T["affT"][:, t * P:(t + 1) * P], ps[0:NE, 5, 0:P]).then_inc(S["affT_taken"], 1)

            def best(b, e, cap, at0, tiles):
                dve.wait_ge(S["affT_taken"], tiles)
                work = T["affT"][:, b:e]
                for r in range(cap // 8):
                    v8, i8 = (T[n][:, at0 + 8 * r:at0 + 8 * r + 8] for n in ("vals", "idx"))
                    own.done(dve.max(v8, work))
                    own.settle()
                    own.done(dve.max_index(i8, v8, work))
                    own.settle()
                    own.done(dve.match_replace(work, v8, work, -1.0))
                    own.settle()

            for t in range(TT + 2):
                if t < TT:
                    residual(t)
                    second_norm(t)
                if t >= 2:
                    affinities(t - 2)
                if t - 2 == TT - 2:
                    best(0, N_LAT, CAP_LAT, 0, TT - 1)
            best(N_LAT, N_TOK, CAP_CTX, CAP_LAT, TT)
            own.done(dve.tensor_copy(T["idx_f"][:], T["idx"][:]))
            own.settle()
            TS(T["idx_f"][:, CAP_LAT:], T["idx_f"][:, CAP_LAT:], float(N_LAT), None, ALU.add).then_inc(S["top_ready"], 1)
            dve.wait_ge(S["topT_done"], 1)
            own.done(dve.tensor_copy(T["val_t"][0:CAP, 0:NE], ps[0:CAP, 6, 0:NE]))
            own.done(dve.tensor_copy(T["idx_t"][0:CAP, 0:NE], ps[0:CAP, 7, 0:NE]))
            own.settle()
            change(dve, 6)

            dve.tensor_copy(T["idx_e"][0:CAP, :], T["idx_t"][0:CAP, 0:1]).then_inc(S["idx_ready"], 1)

            def take_xs(e):
                dve.wait_ge(S["xs_hi_done"], e + 1)
                TTn(xs_lo[:].rearrange("p (b k) n -> p b (k n)", b=4), ps[:, 0:4, 0:4 * CAP],
                    xs_hi[:].rearrange("p (b k) n -> p b (k n)", b=4).bitcast(F32), ALU.subtract
                    ).then_inc(S["xs_lo_done"], 1)

            def expert(e, last):
                quad = Q_EXP + e * 6
                if not last:
                    dve.wait_ge(S["xsT_done"], e + 1)
                    dve.tensor_copy(T["idx_e"][0:CAP, :], T["idx_t"][0:CAP, bass.ds(e + 1, 1)]
                                    ).then_inc(S["idx_ready"], 1)
                for k in range(KT):
                    exp_split_lo(dve, e, k + 1)
                    if k == 9:
                        wait(dve, "ye_free", e)
                        dve.tensor_copy(T["sidx"][0:CAP, :], T["idx_t"][0:CAP, bass.ds(e, 1)])
                        dve.tensor_copy(T["val_e"][0:CAP, :], T["val_t"][0:CAP, bass.ds(e, 1)]
                                        ).then_inc(S["val_set"], 1)
                dve.wait_ge(S["silu_done"], e + 1)
                dve.wait_ge(halves_used, used((quad + 4) * 4))
                h3 = E["hid"][0:CAP, :].rearrange("p (b n) -> p b n", b=2)
                TTn(h3, h3, ps[0:CAP, 2:4, :], ALU.mult).then_inc(S["hid_done"], 1)
                dve.wait_ge(S["hidT_hi"], e + 1)
                TTn(hid_lo[:].rearrange("p (b k) n -> p b (k n)", b=2), ps[:, 4:6, 0:4 * CAP],
                    hid_hi[:].rearrange("p (b k) n -> p b (k n)", b=2).bitcast(F32), ALU.subtract
                    ).then_inc(S["hidT_lo"], 1)
                for k in range(8):
                    if not (last and k == 7):
                        exp_split_lo(dve, e, KT + k + 1)
                    if k == 2 and not last:
                        take_xs(e + 1)
                dve.wait_ge(S["val_set"], e + 1)
                dve.wait_ge(halves_used, used((quad + 6) * 4))
                TS(E["ye"][0:CAP, 1024:].rearrange("p (b n) -> p b n", b=2), ps[0:CAP, 6:8, :],
                   T["val_e"][0:CAP, :], None, ALU.mult).then_inc(S["ye_ready"], 1)

            take_xs(0)
            with dve.Fori(0, NE - 1) as e:
                expert(e, False)
            expert(NE - 1, True)
            change(dve, 7)

            dve.wait_ge(S["g2_loaded"], 32)
            for t in range(TT):
                dve.wait_ge(S["f_sqrt"], t + 1)
                own.done(dve.reciprocal(stats[:, 16 + t:17 + t], stats[:, 8 + t:9 + t]))
                own.settle()
                f = Z["f"][:, t, :]
                own.done(STT(f, f, stats[:, 16 + t:17 + t], G2[:, int(t == TT - 1), :], ALU.mult, ALU.mult))
                own.settle()
                TTn(f, f, t_out[:, t, :], ALU.add).then_inc(S["y_done"], 1)
            dve.wait_ge(S["state_turned"], 1)
            dve.tensor_copy(state_rows[:], ps[0:16, 0, 0:P]).then_inc(S["state_row"], 1)

        @block.tensor
        def _(pe):
            pe.sem_inc(halves_used, 2 * NHL)

            def turn(out, in_, n=P):
                return pe.transpose(out, in_, ident[0:n, 0:n])

            pe.wait_ge(S["c_loaded"], 64)
            turn(ps[:, 7, 0:48], A["rows1"][:], 48).then_inc(S["rows_turned"], 1)

            def turn_x(t):
                pe.wait_ge(S["xn_ready"], t + 1)
                for kq in range(4):
                    if t:
                        pe.wait_ge(S[("xt_act", "xt_dve")[kq % 2]], 2 * (t - 1) + kq // 2 + 1)
                    for k in range(4 * kq, 4 * kq + 4):
                        last = pe.matmul(ps[:, 4 + kq, (k % 4) * P:(k % 4 + 1) * P], x_in[:, t, k * P:(k + 1) * P],
                                         A["diag"][:, t % 2, :], start=True, stop=True)
                    last.then_inc(S["x_turned"], 1)

            def mod_group(g, after=()):
                wait(pe, "m_row_ready", g)
                for k in range(KT):
                    by_halves(pe, Q_MOD * NRAW + g * KT + k, k % 2, ps[0:2, 0:4, :], c_hi[:, k, :], c_lo[:, k, :],
                              k == 0, k == KT - 1)
                    if k in after:
                        after[k]()

            def turn_vectors():
                pe.wait_ge(S["rows3_loaded"], 64)
                turn(ps[:, 7, 0:64], A["rows3"][:], 64).then_inc(S["rows3_turned"], 1)

            def turn_parameters():
                pe.wait_ge(par_loaded, N_PAR * 16)
                turn(ps[:, 7, 128:233], A["rows2"][:], 105).then_inc(S["rows_turned"], 1)

            def spread_lambda():
                pe.wait_ge(S["lam_val"], 1)
                pe.matmul(ps[:, 6, 0:1], A["ones_row"][:], A["lams"][0:1, 5:6], start=True, stop=True
                          ).then_inc(S["lam_spread"], 1)

            pe.wait_ge(S["c_ready"], 1)
            mod_group(0, {8: turn_parameters})
            spread_lambda()
            mod_group(1, {3 * t + 1: (lambda t=t: turn_x(t)) for t in range(TT)})
            mod_group(2, {9: turn_vectors})
            with pe.Fori(3, 6) as g:
                mod_group(g)
            leave(pe)
            wait(pe, "m_row_ready", 6)

            def wide(quad, c, first_bank_free, out_sem, tok_wait):
                for kq in range(4):
                    unit_wait(pe, quad, kq)
                    for kk in range(4):
                        k = 4 * kq + kk
                        tok_wait(k)
                        s = slice(kk * 512, (kk + 1) * 512)
                        for t in range(TT):
                            if k == 0:
                                first_bank_free(t)
                            ts = slice(t * P, (t + 1) * P)
                            last = three(pe, ps[:, t, :], hi[:, k, ts], lo[:, k, ts], w_hi[:, kq % 2, s],
                                         w_lo[:, kq % 2, s], k == 0, k == KT - 1)
                            if k == KT - 1 and t < TT - 1:
                                last.then_inc(out_sem, 1)
                    last.then_inc(halves_used, 2)

            pe.wait_ge(S["tok_lo"], KT)
            with pe.Fori(0, 2) as c:
                wide(Q_V + c, c, lambda t: wait(pe, "bank_taken", c * TT + t + 1 - TT), S["bank_done"], lambda k: None)

            def unit_piece(j, half, ks, bank):
                ms = slice(half * HALF, (half + 1) * HALF)
                for k in ks:
                    s = slice(k * P, (k + 1) * P)
                    wh, wl = w_hi[:, j % 2, s], w_lo[:, j % 2, s]
                    out = ps[:, bank, 0:HALF]
                    pe.matmul(out, wl, hi[:, k, ms], start=(k % 16 == 0), stop=False)
                    pe.matmul(out, wh, lo[:, k, ms], start=False, stop=False)
                    last = pe.matmul(out, wh, hi[:, k, ms], start=False, stop=(k == KT - 1))
                return last

            with pe.Fori(0, 8) as i:
                for j in range(4):
                    unit_wait(pe, Q_IN + i, j)
                    for half in range(2):
                        wait(pe, "in_taken", (i * 4 + j) * 2 + half - 1)
                        last = unit_piece(j, half, range(KT), 5 + half)
                        last.then_inc(*((S["in_a_done"], 1) if half == 0 else (halves_used, 2)))
            leave(pe)
            wait(pe, "bank_taken", 2 * TT)
            wait(pe, "in_taken", 2 * 32)

            with pe.Fori(0, NH) as h:
                def keys():
                    pe.wait_ge(S["kp_loaded"], h * 16 + 16)
                    pe.wait_ge(S["k_loaded"], h * 16 + 16)
                    wait(pe, "pdT_taken", h * TT)
                    turn(ps[:, 4, 0:P], C["k_past"][:])
                    turn(ps[:, 7, 0:P], C["k"][:, N_LAT:]).then_inc(S["kt_done"], 1)
                    pe.wait_ge(S["rope_loaded"], 32)
                    pe.wait_ge(S["q_loaded"], h * 16 + 16)
                    wait(pe, "o_ready", h * 2)
                    for i, x in enumerate((C["k"], C["q_in"])):
                        pe.matmul(ps[:, i, :], C["perm"][:], x[:, 0:N_LAT], start=True, stop=True
                                  ).then_inc(S["rot_done"], 1)

                def lru(d):
                    if d == 0:
                        pe.wait_ge(S["xc_ready"], h + 1)
                        pe.wait_ge(S["lruw_loaded"], h * 32 + 32)
                        pe.wait_ge(S["rot_read"], h * 2 + 2)
                    else:
                        pe.wait_ge(S["lru_sig"], h * 4 + 2)
                    for i in range(2):
                        for half in range(2):
                            last = pe.matmul(ps[:, 2 * i + half, 0:HALF], C["lru_w"][:, 2 * d + i, :],
                                             C["xc"][:, half * HALF:(half + 1) * HALF], start=True, stop=True)
                    last.then_inc(S["lru_mm"], 1)

                def scores(qt):
                    if qt == 0:
                        pe.wait_ge(S["lru_sig"], h * 4 + 4)
                        pe.wait_ge(S["qk_ready"], h * 4 + 4)
                    else:
                        pe.wait_ge(S["score_exp"], h * 2 * TT + 2 * qt)
                    for c in range(2):
                        rows = slice(c * HD, (c + 1) * HD)
                        q = C["q"][rows, qt * P:(qt + 1) * P]
                        if qt < TT - 1:
                            for half in range(2):
                                last = pe.matmul(ps[:, 2 * c + half, 0:HALF], q,
                                                 C["k_all"][rows, half * HALF:(half + 1) * HALF], start=True, stop=True)
                        else:
                            last = pe.matmul(ps[:, 2 * c, 0:P], q, C["k_all"][rows, NKEY:], start=True, stop=True)
                    last.then_inc(S["score_done"], 1)

                def turn_probs(qt):
                    pe.wait_ge(S["pd_ready"], h * TT + qt + 1)
                    if qt == 0:
                        pe.wait_ge(S["kt_taken"], h * 2 + 2)
                    else:
                        wait(pe, "pdT_taken", h * TT + qt)
                    p = C["probs"][:, qt % 2, 0, :]
                    for kt in range(5 if qt < TT - 1 else 1):
                        out = ps[:, 4, kt * P:(kt + 1) * P] if kt < 4 else ps[:, 7, 0:P]
                        last = turn(out, p[:, kt * P:(kt + 1) * P])
                    last.then_inc(S["pdT_done"], 1)

                def values():
                    wait(pe, "pdT_taken", h * TT + TT)
                    pe.wait_ge(S["v_loaded"], h * 32 + 32)
                    for kt in range(TT):
                        pe.matmul(ps[:, 0, :], C["v"][:, kt, :], C["pT"][:, kt, :], start=(kt == 0), stop=(kt == TT - 1))
                    pe.matmul(ps[:, 1, 0:P], C["v"][:, TT, :], C["pT_ctx"][:], start=True, stop=True
                              ).then_inc(S["av_done"], 1)

                def mean_square():
                    pe.wait_ge(S["o_sq"], h + 1)
                    pe.matmul(ps[:, 2, :], mean_mat[:], C["probs"][:, 0, 0, 0:N_LAT], start=True, stop=True)
                    pe.matmul(ps[:, 3, 0:P], mean_mat[:], C["probs"][:, 0, 0, N_LAT:], start=True, stop=True
                              ).then_inc(S["ms_done"], 1)

                after = {2: [keys], 3: [lambda: lru(0)], 4: [lambda: lru(1)], 7: [lambda: scores(0)],
                         9: [lambda: scores(1)], 10: [lambda: turn_probs(0), lambda: scores(2)],
                         11: [lambda: turn_probs(1), lambda: scores(3)], 12: [lambda: turn_probs(2), lambda: scores(4)],
                         13: [lambda: turn_probs(3), lambda: turn_probs(4)], 14: [values], 15: [mean_square]}
                for piece in range(16):
                    j, half, part = piece // 4, piece % 4 // 2, piece % 2
                    if part == 0:
                        if half == 0:
                            unit_wait(pe, Q_GATE + h, j)
                        wait(pe, "gate_taken", (h * 4 + j) * 2 + half - 1)
                    last = unit_piece(j, half, range(8 * part, 8 * part + 8), 5 + half)
                    if part == 1:
                        last.then_inc(*((S["gate_a_done"], 1) if half == 0 else (halves_used, 2)))
                    for step in after.get(piece, []):
                        step()
            leave(pe)
            wait(pe, "o_ready", 2 * NH)

            with pe.Fori(0, 4) as i:
                for j in range(4):
                    unit_wait(pe, Q_AB + i, j)
                    wait(pe, "mix_done", i * 4 + j - 1)
                    for br in range(2):
                        for half in range(2):
                            ms = slice(half * HALF, (half + 1) * HALF)
                            out = ps[:, 4 * (j % 2) + 2 * br + half, 0:HALF]
                            for k in range(8 * br, 8 * br + 8):
                                if j == 0 and half == 0:
                                    pe.wait_ge(S["split_in_lo"], k + 1)
                                s = slice(k * P, (k + 1) * P)
                                wh, wl = w_hi[:, j % 2, s], w_lo[:, j % 2, s]
                                pe.matmul(out, wl, hi[:, k, ms], start=(k % 8 == 0), stop=False)
                                pe.matmul(out, wh, lo[:, k, ms], start=False, stop=False)
                                last = pe.matmul(out, wh, hi[:, k, ms], start=False, stop=(k % 8 == 7))
                        last.then_inc(*((S["ab_a"], 1) if br == 0 else (halves_used, 2)))
            leave(pe)
            wait(pe, "mix_done", KT)

            for c in range(4):
                wide(Q_O + c, c, lambda t: wait(pe, "o_taken", (c - 1) * TT + t + 1), S["bank_done"],
                     lambda k: pe.wait_ge(S["split_in_lo"], KT + k + 1) if c == 0 else None)
            change(pe, 5)

            def turn_affinities(t):
                pe.wait_ge(S["aff_ready"], t + 1)
                if t:
                    pe.wait_ge(S["affT_taken"], t)
                turn(ps[0:NE, 5, 0:P], T["aff"][:]).then_inc(S["affT_done"], 1)

            pe.wait_ge(S["wr_loaded"], 16)
            for t in range(TT + 1):
                if t < TT:
                    pe.wait_ge(S["h2_ready"], t + 1)
                    for k in range(KT):
                        last = turn(ps[:, k // 4, (k % 4) * P:(k % 4 + 1) * P],
                                    R2["h2"][:, t % 2, k * P:(k + 1) * P])
                    last.then_inc(S["h2T_done"], 1)
                    pe.wait_ge(S["h2T_taken"], t + 1)
                    if t == TT - 1:
                        turn_affinities(t - 1)
                    if t >= 2:
                        pe.wait_ge(S["logit_exp"], t - 1)
                    for k in range(KT):
                        last = pe.matmul(ps[:, 4 + 2 * (t % 2), 0:NE], R2["h2T"][:, k, :], T["wr"][:, k, :],
                                         start=(k == 0), stop=(k == KT - 1))
                    last.then_inc(S["logit_done"], 1)
                if t and t != TT - 1:
                    turn_affinities(t - 1)
            pe.wait_ge(S["top_ready"], 1)
            turn(ps[0:CAP, 6, 0:NE], T["vals"][:], NE)
            turn(ps[0:CAP, 7, 0:NE], T["idx_f"][:], NE).then_inc(S["topT_done"], 1)
            change(pe, 6)

            def turn_xs(e):
                pe.wait_ge(S["gathered"], e * 16 + 16)
                for k in range(KT):
                    last = turn(ps[:, k // 4, (k % 4) * CAP:(k % 4 + 1) * CAP], E["xs"][0:CAP, k * P:(k + 1) * P], CAP)
                last.then_inc(S["xsT_done"], 1)

            def expert(e, last_one):
                quad = Q_EXP + e * 6
                pe.wait_ge(S["xs_lo_done"], e + 1)
                for k in range(KT):
                    by_halves(pe, quad * 4 + k, k % 2, ps[0:CAP, 0:4, :], xs_hi[:, k, :], xs_lo[:, k, :],
                              k == 0, k == KT - 1)
                pe.wait_ge(S["hid_done"], e + 1)
                wait(pe, "ye_ready", 2 * e)
                for k in range(8):
                    last = turn(ps[:, 4 + k // 4, (k % 4) * CAP:(k % 4 + 1) * CAP],
                                E["hid"][0:CAP, k * P:(k + 1) * P], CAP)
                last.then_inc(S["hidT_done"], 1)
                pe.wait_ge(S["hidT_lo"], e + 1)
                for k in range(8):
                    by_halves(pe, quad * 4 + KT + k, k % 2, ps[0:CAP, 4:8, :], hid_hi[:, k, :], hid_lo[:, k, :],
                              k == 0, k == 7)
                    if k == 1 and not last_one:
                        turn_xs(e + 1)

            turn_xs(0)
            with pe.Fori(0, NE - 1) as e:
                expert(e, False)
            expert(NE - 1, True)
            change(pe, 7)
            turn(ps[0:16, 0, 0:P], state_col[:]).then_inc(S["state_turned"], 1)


_INS = ["x_prompt", "x_sample", "cache_k", "cache_v", "state_rnn", "c", "c_ctx", "w_mod", "b_mod", "g_pre1", "g_post1",
        "g_pre2", "g_post2", "w_in", "conv_w", "conv_b", "lru_wr", "lru_br", "lru_wi", "lru_bi", "lru_lam", "lam_q1",
        "lam_k1", "lam_q2", "lam_k2", "g_sub", "w_a_out", "w_b_out", "w_o", "w_router", "w_e_gate", "w_e_up",
        "w_e_down"]
_OUTS = [(1, N_CTX, D), (1, N_LAT, D), (1, 1, N_CTX, NH, 2 * HD), (1, 1, N_CTX, NH, 2 * HD), (1, 1, 2, D_RNN)]


def kernel(**inputs):
    import concourse.bacc as bacc
    from concourse.bass_utils import run_bass_kernel_spmd

    nc = bacc.Bacc("TRN2", target_bir_lowering=False, num_devices=1)
    given = {n: np.ascontiguousarray(inputs[n]) for n in _INS}
    given["rope"] = rope_tables()
    given["ident"] = np.eye(P, dtype=np.float32)
    given["perm"] = given["ident"][np.arange(P) ^ (HD // 2)]
    arrays, aps = {}, {}
    for n, x in given.items():
        arrays[f"in_{n}"] = x
        aps[n] = nc.dram_tensor(f"in_{n}", x.shape, mybir.dt.from_np(x.dtype), kind="ExternalInput").ap()
    outs = [nc.dram_tensor(f"out_{i}", s, F32, kind="ExternalOutput").ap() for i, s in enumerate(_OUTS)]
    trunk(nc, aps, *outs)
    r = run_bass_kernel_spmd(nc, [arrays], core_ids=[0])
    return tuple(r.results[0][f"out_{i}"] for i in range(len(_OUTS)))
```
